# Optimizing a Trainium2 kernel written in Bass

```python
import jax, jax.numpy as jnp
from jax import lax
import numpy as np

D_MODEL = 2048
BATCH = 1
SEQ = 256
DEPTH = 1

GRID_W = 64
GLA_HEADS = 4
GLA_DK = D_MODEL // 4
GLA_DV = D_MODEL // 2
GLA_HK = GLA_DK // GLA_HEADS
GLA_HV = GLA_DV // GLA_HEADS
GLA_GATE_RANK = 16
GLA_TAU = 16.0
GLA_CHUNK = 64
NA_HD = 64
NA_WIDTH = D_MODEL // 4
NA_HEADS = NA_WIDTH // NA_HD
NA_ROWS = 8
NA_COLS = 16
NA_QB_W = 16
NA_KB_W = NA_QB_W + NA_COLS
MEM_TOKENS = 256
MEM_HEADS = 4
MEM_WIDTH = D_MODEL // 4
MEM_HD = MEM_WIDTH // MEM_HEADS
MIX_WIDTH = GLA_DV + NA_WIDTH + MEM_WIDTH
IN_SPLITS = (GLA_DK, GLA_DK, GLA_DV, GLA_DV, GLA_GATE_RANK, GLA_GATE_RANK,
             NA_WIDTH, NA_WIDTH, NA_WIDTH, MEM_WIDTH)
IN_COLS = sum(IN_SPLITS)
D_FF = ((8 * D_MODEL // 3 + 255) // 256) * 256
RMS_EPS = 1e-6

kernel_name = "hybrid_gla_natten_mem_encoder"

def rms_norm(x, g):
    xf = x.astype(jnp.float32)
    y = xf * lax.rsqrt(jnp.mean(xf * xf, axis=-1, keepdims=True) + RMS_EPS)
    return (y * g.astype(jnp.float32)).astype(x.dtype)

def head_rms_norm(t, g, n_heads):
    B, S, W = t.shape
    y = rms_norm(t.reshape(B, S, n_heads, W // n_heads), g.reshape(n_heads, W // n_heads))
    return y.reshape(B, S, W)

def split_heads(t, n_heads):
    B, S, W = t.shape
    return t.reshape(B, S, n_heads, W // n_heads).transpose(0, 2, 1, 3)

def merge_heads(t):
    B, H, S, d = t.shape
    return t.transpose(0, 2, 1, 3).reshape(B, S, H * d)

def gla_chunked(q, k, v, log_a, strict):
    B, H, S, dk = q.shape
    dv = v.shape[-1]
    C = GLA_CHUNK
    N = S // C
    qc = q.astype(jnp.float32).reshape(B, H, N, C, dk)
    kc = k.astype(jnp.float32).reshape(B, H, N, C, dk)
    vc = v.astype(jnp.float32).reshape(B, H, N, C, dv)
    cum = jnp.cumsum(log_a.astype(jnp.float32).reshape(B, H, N, C, dk), axis=3)
    last = cum[:, :, :, -1:, :]
    q_e = qc * jnp.exp(cum)
    k_e = kc * jnp.exp(-cum)
    k_end = kc * jnp.exp(last - cum)
    scores = jnp.einsum('bhnqd,bhnkd->bhnqk', q_e, k_e)
    mask = np.tril(np.ones((C, C), dtype=bool), k=-1 if strict else 0)
    scores = jnp.where(mask, scores, 0.0)
    o_intra = jnp.einsum('bhnqk,bhnke->bhnqe', scores, vc)
    kv = jnp.einsum('bhnkd,bhnke->nbhde', k_end, vc)
    decay = jnp.exp(last[:, :, :, 0, :]).transpose(2, 0, 1, 3)

    def step(state, inp):
        dec, kv_n = inp
        return dec[..., None] * state + kv_n, state

    _, s_prev = lax.scan(step, jnp.zeros((B, H, dk, dv), jnp.float32), (decay, kv))
    o_inter = jnp.einsum('bhnqd,nbhde->bhnqe', q_e, s_prev)
    return (o_intra + o_inter).reshape(B, H, S, dv)

def gla_group(q_in, k_in, v_in, r_in, gf_in, gb_in, wg2_f, bg_f, wg2_b, bg_b, out_norm):
    q = split_heads(q_in, GLA_HEADS) * (GLA_HK ** -0.5)
    k = split_heads(k_in, GLA_HEADS)
    v = split_heads(v_in, GLA_HEADS)
    z_f = gf_in.astype(jnp.float32) @ wg2_f.astype(jnp.float32) + bg_f.astype(jnp.float32)
    z_b = gb_in.astype(jnp.float32) @ wg2_b.astype(jnp.float32) + bg_b.astype(jnp.float32)
    la_f = split_heads(jax.nn.log_sigmoid(z_f) / GLA_TAU, GLA_HEADS)
    la_b = split_heads(jax.nn.log_sigmoid(z_b) / GLA_TAU, GLA_HEADS)
    o_f = gla_chunked(q, k, v, la_f, strict=False)
    flip = lambda t: jnp.flip(t, axis=2)
    o_b = flip(gla_chunked(flip(q), flip(k), flip(v), flip(la_b), strict=True))
    o = merge_heads(o_f + o_b).astype(q_in.dtype)
    o = head_rms_norm(o, out_norm, GLA_HEADS)
    return o * jax.nn.silu(r_in)

def natten2d(q, k, v, rpb):
    B, H, S, dh = q.shape
    rows = S // GRID_W
    kr = min(NA_ROWS, rows)
    nj = GRID_W // NA_QB_W
    r = np.arange(rows)
    rs = np.clip(r - kr // 2, 0, rows - kr)
    c0 = np.arange(nj) * NA_QB_W
    kc0 = np.clip(c0 - NA_COLS // 2, 0, GRID_W - NA_KB_W)
    key_rows = rs[:, None] + np.arange(kr)[None, :]
    key_cols = kc0[:, None] + np.arange(NA_KB_W)[None, :]
    nk = kr * NA_KB_W
    idx = (key_rows[:, None, :, None] * GRID_W + key_cols[None, :, None, :]).reshape(-1)
    k_blk = jnp.take(k, idx, axis=2).reshape(B, H, rows, nj, nk, dh)
    v_blk = jnp.take(v, idx, axis=2).reshape(B, H, rows, nj, nk, dh)
    q_blk = q.reshape(B, H, rows, nj, NA_QB_W, dh)
    qcol = c0[:, None] + np.arange(NA_QB_W)[None, :]
    cs = np.clip(qcol - NA_COLS // 2, 0, GRID_W - NA_COLS)
    in_win = (key_cols[:, None, :] >= cs[:, :, None]) & (key_cols[:, None, :] < cs[:, :, None] + NA_COLS)
    mask = np.broadcast_to(in_win[:, :, None, :], (nj, NA_QB_W, kr, NA_KB_W)).reshape(nj, NA_QB_W, nk)
    dr = key_rows - r[:, None] + (NA_ROWS - 1)
    dc = np.clip(key_cols[:, None, :] - qcol[:, :, None], -(NA_COLS - 1), NA_COLS - 1) + (NA_COLS - 1)
    bias = rpb[:, dr[:, None, None, :, None], dc[None, :, :, None, :]].reshape(H, rows, nj, NA_QB_W, nk)
    s = jnp.einsum('bhrjqd,bhrjkd->bhrjqk', q_blk, k_blk).astype(jnp.float32) * (dh ** -0.5)
    s = s + bias[None].astype(jnp.float32)
    s = jnp.where(mask, s, -jnp.inf)
    p = jax.nn.softmax(s, axis=-1).astype(v.dtype)
    o = jnp.einsum('bhrjqk,bhrjkd->bhrjqd', p, v_blk)
    return o.reshape(B, H, S, dh)

def natten_group(q_in, k_in, v_in, q_norm, k_norm, rpb, out_norm):
    q = rms_norm(split_heads(q_in, NA_HEADS), q_norm)
    k = rms_norm(split_heads(k_in, NA_HEADS), k_norm)
    v = split_heads(v_in, NA_HEADS)
    o = merge_heads(natten2d(q, k, v, rpb))
    return head_rms_norm(o, out_norm, NA_HEADS)

def memory_group(q_in, mem, mem_norm, mem_wkv, q_norm, k_norm, out_norm):
    q = rms_norm(split_heads(q_in, MEM_HEADS), q_norm)
    kv = rms_norm(mem, mem_norm) @ mem_wkv
    k_m, v_m = jnp.split(kv, 2, axis=-1)
    k_m = rms_norm(split_heads(k_m, MEM_HEADS), k_norm)
    v_m = split_heads(v_m, MEM_HEADS)
    s = jnp.einsum('bhqd,bhkd->bhqk', q, k_m).astype(jnp.float32) * (MEM_HD ** -0.5)
    p = jax.nn.softmax(s, axis=-1).astype(v_m.dtype)
    o = merge_heads(jnp.einsum('bhqk,bhkd->bhqd', p, v_m))
    return head_rms_norm(o, out_norm, MEM_HEADS)

def setup_inputs(seed: int = 0) -> dict:
    key = jax.random.key(seed)
    ks = jax.random.split(key, 22)
    f32 = jnp.float32

    def nrm(k, shape, scale):
        return jax.random.normal(k, shape, f32) * scale

    def gain(k, shape):
        return 1.0 + 0.05 * jax.random.normal(k, shape, f32)

    out_scale = (2 * DEPTH) ** -0.5
    return {
        "x": nrm(ks[0], (BATCH, SEQ, D_MODEL), 1.0),
        "mem": nrm(ks[1], (BATCH, MEM_TOKENS, D_MODEL), 1.0),
        "attn_norm": gain(ks[2], (DEPTH, D_MODEL)),
        "w_in": nrm(ks[3], (DEPTH, D_MODEL, IN_COLS), D_MODEL ** -0.5),
        "gla_wg2_f": nrm(ks[4], (DEPTH, GLA_GATE_RANK, GLA_DK), GLA_GATE_RANK ** -0.5),
        "gla_bg_f": nrm(ks[5], (DEPTH, GLA_DK), 0.1),
        "gla_wg2_b": nrm(ks[6], (DEPTH, GLA_GATE_RANK, GLA_DK), GLA_GATE_RANK ** -0.5),
        "gla_bg_b": nrm(ks[7], (DEPTH, GLA_DK), 0.1),
        "gla_out_norm": gain(ks[8], (DEPTH, GLA_DV)),
        "na_q_norm": gain(ks[9], (DEPTH, NA_HD)),
        "na_k_norm": gain(ks[10], (DEPTH, NA_HD)),
        "na_rpb": nrm(ks[11], (DEPTH, NA_HEADS, 2 * NA_ROWS - 1, 2 * NA_COLS - 1), 0.1),
        "na_out_norm": gain(ks[12], (DEPTH, NA_WIDTH)),
        "mem_norm": gain(ks[13], (DEPTH, D_MODEL)),
        "mem_wkv": nrm(ks[14], (DEPTH, D_MODEL, 2 * MEM_WIDTH), D_MODEL ** -0.5),
        "mem_q_norm": gain(ks[15], (DEPTH, MEM_HD)),
        "mem_k_norm": gain(ks[16], (DEPTH, MEM_HD)),
        "mem_out_norm": gain(ks[17], (DEPTH, MEM_WIDTH)),
        "w_out": nrm(ks[18], (DEPTH, MIX_WIDTH, D_MODEL), MIX_WIDTH ** -0.5 * out_scale),
        "ffn_norm": gain(ks[19], (DEPTH, D_MODEL)),
        "ffn_w13": nrm(ks[20], (DEPTH, D_MODEL, 2 * D_FF), D_MODEL ** -0.5),
        "ffn_w2": nrm(ks[21], (DEPTH, D_FF, D_MODEL), D_FF ** -0.5 * out_scale),
    }

def reference(x, mem, attn_norm, w_in, gla_wg2_f, gla_bg_f, gla_wg2_b, gla_bg_b, gla_out_norm,
              na_q_norm, na_k_norm, na_rpb, na_out_norm, mem_norm, mem_wkv, mem_q_norm, mem_k_norm,
              mem_out_norm, w_out, ffn_norm, ffn_w13, ffn_w2):
    split_points = np.cumsum(IN_SPLITS)[:-1].tolist()
    for l in range(DEPTH):
        xn = rms_norm(x, attn_norm[l])
        proj = xn @ w_in[l]
        (g_q, g_k, g_v, g_r, g_f, g_b, n_q, n_k, n_v, m_q) = jnp.split(proj, split_points, axis=-1)
        y_gla = gla_group(g_q, g_k, g_v, g_r, g_f, g_b, gla_wg2_f[l], gla_bg_f[l],
                          gla_wg2_b[l], gla_bg_b[l], gla_out_norm[l])
        y_na = natten_group(n_q, n_k, n_v, na_q_norm[l], na_k_norm[l], na_rpb[l], na_out_norm[l])
        y_mem = memory_group(m_q, mem, mem_norm[l], mem_wkv[l], mem_q_norm[l], mem_k_norm[l],
                             mem_out_norm[l])
        x = x + jnp.concatenate([y_gla, y_na, y_mem], axis=-1) @ w_out[l]
        h = rms_norm(x, ffn_norm[l])
        gate, up = jnp.split(h @ ffn_w13[l], 2, axis=-1)
        x = x + (jax.nn.silu(gate) * up) @ ffn_w2[l]
    return x


_drawn_inputs = setup_inputs


def setup_inputs(seed=0):
    import zlib

    import numpy as np

    out = dict(_drawn_inputs(seed))
    spreads = {}
    factors = {'gla_wg2_f': 2.669,
     'gla_bg_f': 6.602,
     'gla_wg2_b': 2.78,
     'gla_bg_b': 6.859,
     'gla_out_norm': 4.384,
     'na_q_norm': 3.527,
     'na_k_norm': 3.484,
     'na_out_norm': 3.57,
     'mem_q_norm': 3.702,
     'mem_k_norm': 3.526,
     'mem_out_norm': 3.632,
     'na_rpb': 3.405,
     'ffn_norm': 4.756}
    for name, (base, spread) in spreads.items():
        noise = np.random.default_rng([zlib.crc32(name.encode()), seed]).standard_normal(out[name].shape)
        drawn = base * np.exp(spread * noise) if base else spread * noise
        out[name] = __import__('jax').numpy.asarray(drawn.astype(out[name].dtype))
    for name, factor in factors.items():
        out[name] = (out[name] * factor).astype(out[name].dtype)
    return out
```

```python
from contextlib import ExitStack

import concourse.bass as bass
from concourse import mybir

F32 = mybir.dt.float32
F32R = mybir.dt.float32r
I32 = mybir.dt.int32
ALU = mybir.AluOpType
ACT = mybir.ActivationFunctionType
AX = mybir.AxisListType.X

P = 128
NT = 2
T = NT * P
D = 2048
KT = D // P
CH = 512
GH, GK, GV = 4, 128, 256
GC, NCH = 64, 4
RANK = 16
TAU = 16.0
NH, ND = 8, 64
NROW, GW = 4, 64
RB_R, RB_C = 15, 31
WIN = 16
MH, MD = 4, 128
DFF = 5632
FC = DFF // CH
EPS = 1e-6
MASKED = -1e30

RAW_SLOTS = 3
UNIT_SLOTS = 3

PQ, PK, PV, PR, NQ, NK, NV, MQ = 0, 512, 1024, 2048, 3072, 3584, 4096, 4608
PCOLS = 5120
WQ, WK, WV, WR, WG = 0, 512, 1024, 2048, 3072
WNQ, WNK, WNV, WMQ = 3104, 3616, 4128, 4640
V_ATTN, V_MEM, V_FFN, V_OUT, V_BGF, V_BGB, V_NQ, V_NK, V_MQ, V_MK, V_ROWS = 0, 16, 32, 48, 64, 68, 72, 73, 74, 75, 76

CHUNKS = [
    (False, WQ, "proj", PQ), (False, WK, "proj", PK), (False, WV, "proj", PV), (False, WV + CH, "proj", PV + CH),
    (False, WNQ, "proj", NQ), (False, WNK, "proj", NK), (True, 0, "kvm", 0), (False, WNV, "proj", NV),
    (False, WMQ, "proj", MQ), (True, CH, "kvm", CH), (False, WR, "proj", PR), (False, WR + CH, "proj", PR + CH),
]
OUT_PIECES = [(0, 8), (0, 0), (1, 8), (1, 0), (0, 12), (0, 4), (1, 12), (1, 4)] + [
    (c, k) for c in (2, 3) for k in (8, 0, 12, 4)]
U_OUT = 8 * len(CHUNKS)
U_FFN = U_OUT + 2 * len(OUT_PIECES)
U_BODY = U_FFN + 16
BODY = 24
U_TAIL = U_BODY + BODY * (FC - 1)

MEM_BANKS = (6, 7, 5)
DOWN_BANKS = (4, 0, 6, 4)

GLA_AT = [20 + 8 * h for h in range(GH)]
ATT_AT = [65 + 2 * h for h in range(NH)] + [82 + 2 * h for h in range(MH)]
NORMS = [("proj", NQ, ND, 44, 48), ("proj", NK, ND, 52, 56), ("kvm", 0, MD, 60, 65), ("proj", MQ, MD, 76, 79)]
ONORMS = [(NQ, ND, 91, 94), (MQ, MD, 100, 103)]
X1_AT = [(111, 110, 113), (115, 114, 117), (123, 122, 125), (131, 130, 133)]


def build_layer(nc, x, mem, attn_norm, w_in, wg2_f, bg_f, wg2_b, bg_b, gla_out, na_q, na_k, rpb, na_out,
                mem_norm, wkv, mem_q, mem_k, mem_out, w_out, ffn_norm, w13, w2, out):
    PADC = P
    bias_rows = nc.dram_tensor("bias_rows", [NH, RB_R, PADC], F32, kind="Internal")

    with ExitStack() as ctx:
        def sb(name, shape, dt=F32):
            return ctx.enter_context(nc.sbuf_tensor(name, shape, dt))

        def sem(name):
            return ctx.enter_context(nc.semaphore(name))

        xin = sb("xin", [P, NT, D])
        A_hi = sb("A_hi", [P, KT, T], F32R)
        A_lo = sb("A_lo", [P, KT, T], F32R)
        B_hi = sb("B_hi", [P, KT, T], F32R)
        B_lo = sb("B_lo", [P, KT, T], F32R)
        proj = sb("proj", [P, NT, PCOLS])
        kvm = sb("kvm", [P, NT, 2 * CH])
        raw = sb("raw", [P, RAW_SLOTS, 4, CH])
        w_hi = sb("w_hi", [P, UNIT_SLOTS, 2, CH], F32R)
        w_lo = sb("w_lo", [P, UNIT_SLOTS, 2, CH], F32R)
        work = sb("work", [P, 6272])
        ident = sb("ident", [P, P])
        masks = sb("masks", [P, 2, NT, P], I32)
        vrow = sb("vrow", [V_ROWS, P])
        vcol = sb("vcol", [P, V_ROWS])
        colmask = sb("colmask", [P, GW])
        resets = sb("resets", [P, 2, 2 * GC])
        small = sb("small", [P, 256])
        ps = ctx.enter_context(nc.psum_tensor("ps", [P, 8, CH], F32))

        def wk(at, n):
            return work[:, at:at + n]

        def dirs(ap):
            return ap.rearrange("p (d t) -> p d t", d=2)

        softp, la, cum, e_pos, e_neg, q_e, k_e, k_end = (dirs(wk(512 * i, 512)) for i in range(8))
        k_tok = wk(4096, 512).rearrange("p (d t k) -> p d t k", d=2, t=NT)
        states = wk(4608, 1536).rearrange("p (d n v) -> p d n v", d=2, n=3)
        scores = wk(0, 1024).rearrange("p (b t k) -> p b t k", b=2, t=NT)
        probs = wk(1024, 1024).rearrange("p (b t k) -> p b t k", b=2, t=NT)
        probsT = wk(2048, 1024).rearrange("p (b k q) -> p b k q", b=2, k=NT)
        na_qT = wk(3072, 1024).rearrange("p (j t) -> p j t", j=4)
        na_kT = wk(4608, 1024).rearrange("p (j t) -> p j t", j=4)
        osq = wk(3072, 1024).rearrange("p (t c) -> p t c", t=NT)
        h_tok = wk(0, 1024).rearrange("p (t c) -> p t c", t=NT)
        silu_g = wk(1024, 1024).rearrange("p (t c) -> p t c", t=NT)
        scoresT = sb("scoresT", [P, NT, P])
        gate_raw = proj[:, 0, PR + CH:PR + 2 * CH].rearrange("p (k c) -> p k c", c=2 * RANK)
        wg2 = proj[0:RANK, 0:2, PR:PR + CH]
        gT = proj[0:RANK, 0, MQ:MQ + CH].rearrange("p (d t) -> p d t", d=2)
        gates_raw = proj[0:4 * RANK, 1, MQ:MQ + T]
        mem_qT = proj[:, 0, 0:1024].rearrange("p (j t) -> p j t", j=4)
        mem_kT = proj[:, 1, 0:1024].rearrange("p (j t) -> p j t", j=4)
        bias = [proj[:, b, PR:PR + CH].rearrange("p (t k) -> p t k", t=NT) for b in range(2)]
        bias_rev = [proj[:, b, PR + CH:PR + 2 * CH].rearrange("p (a c) -> p a c", c=GW) for b in range(2)]
        row_scratch = kvm[:].rearrange("p t c -> p (t c)")
        psq = kvm[:, :, CH:2 * CH]
        gate_hi = B_hi[:].rearrange("p a b -> p (a b)")[:, 0:(KT + 1) * 4 * RANK]
        gate_lo = B_lo[:].rearrange("p a b -> p (a b)")[:, 0:(KT + 1) * 4 * RANK]
        pad = wk(6144, PADC)[0:NH * RB_R, :]
        rpb_sb = sb("rpb_sb", [NH * RB_R, RB_C])

        ssq_x, rstd_x = small[:, 0:2], small[:, 2:4]
        ssq_m, rstd_m = small[:, 4:6], small[:, 6:8]
        ssq_o, rstd_o = small[:, 8:16], small[:, 16:24]
        ssq_n = [small[:, 24 + 16 * i:40 + 16 * i] for i in range(6)]
        rstd_n = [small[:, 120 + 16 * i:136 + 16 * i] for i in range(6)]
        ssq_h, sum_h, rstd_h = small[:, 216:224], small[:, 224:226], small[:, 226:228]
        stat = sb("stat", [P, 128])
        negmax = stat[:, 64:68].rearrange("p (b t) -> p b t", b=2)
        psum_e = stat[:, 68:92].rearrange("p (g t) -> p g t", t=NT)
        rinv = stat[:, 92:116].rearrange("p (g t) -> p g t", t=NT)
        half = sb("half", [P, 16])

        raw_landed = [sem(f"raw_landed{i}") for i in range(RAW_SLOTS)]
        hi_ready = sem("hi_ready")
        lo_ready = sem("lo_ready")
        unit_done = sem("unit_done")
        x_landed, mem_landed, x_again = [sem(f"x_landed{c}") for c in range(4)], sem("mem_landed"), sem("x_again")
        gain_landed, vec_landed, gate_landed, wg2_landed = sem("gain_landed"), sem("vec_landed"), sem("gate_landed"), sem("wg2_landed")
        rpb_landed, rows_stored, rev_landed = sem("rpb_landed"), sem("rows_stored"), [sem("rev_landed0"), sem("rev_landed1")]
        out_stored = sem("out_stored")
        ident_ready, pad_ready, masks_ready = sem("ident_ready"), sem("pad_ready"), sem("masks_ready")
        vecT, vcol_ready = sem("vecT"), sem("vcol_ready")
        xT, xT_hi, xT_lo = sem("xT"), sem("xT_hi"), sem("xT_lo")
        mT, mT_hi, mT_lo = sem("mT"), sem("mT_hi"), sem("mT_lo")
        x_squared, m_squared = sem("x_squared"), sem("m_squared")
        rstd_x_ready, rstd_m_ready = sem("rstd_x_ready"), sem("rstd_m_ready")
        gate_hi_ready, gate_lo_ready = sem("gate_hi_ready"), sem("gate_lo_ready")
        gates_done, gates_evac, rstd_rows, gT_ready = (sem(n) for n in "gates_done gates_evac rstd_rows gT_ready".split())
        chunk_evac = sem("chunk_evac")
        g_qkT, g_z, g_abs, g_soft, g_cum, g_exp, g_gated = (sem("g_" + n) for n in
                                                            "qkT z abs soft cum exp gated".split())
        g_scores, g_kendT, g_ktok, g_masked, g_kv, g_kvx, g_state, g_o, g_oevac = (
            sem("g_" + n) for n in "scores kendT ktok masked kv kvx state o oevac".split())
        rstd_o_ready = sem("rstd_o_ready")
        n_squared, n_summed, n_rstd, n_scaled = (sem("n_" + n) for n in "squared summed rstd scaled".split())
        headT, headT_evac = sem("headT"), sem("headT_evac")
        bias_ready = sem("bias_ready")
        a_scored, a_copied, a_max, a_exp, a_pT, a_pTevac, a_pv, a_out = (
            sem("a_" + n) for n in "scored copied max exp pT pTevac pv out".split())
        y_ready, yT, yT_hi, yT_lo = sem("y_ready"), sem("yT"), sem("yT_hi"), sem("yT_lo")
        x1_squared, x1T, x1T_hi, x1T_lo = (sem("x1_" + n) for n in "squared T hi lo".split())
        sum_h_ready, rstd_h_ready = sem("sum_h_ready"), sem("rstd_h_ready")
        gate_read, h_ready, hT, hT_hi, hT_lo = (sem(n) for n in "gate_read h_ready hT hT_hi hT_lo".split())
        col_added = sem("col_added")
        act_step, dve_step, pool_step = sem("act_step"), sem("dve_step"), sem("pool_step")
        block = ctx.enter_context(nc.Block())

        def linker(eng, step):
            done = [0]

            def link(ins):
                done[0] += 1
                ins.then_inc(step, 1)
                eng.wait_ge(step, done[0])
            return link

        def acc(pair):
            return ps[:, 2 * pair:2 * pair + 2, :]

        def rows(w, r, c):
            return w[bass.ds(r, 4 * P) if not isinstance(r, int) else slice(r, r + 4 * P),
                     bass.ds(c, CH) if not isinstance(c, int) else slice(c, c + CH)].rearrange("(k p) n -> p k n", p=P)

        def gate_tiles(buf):
            v = buf.rearrange("p (k a r) -> p k a r", a=2, r=RANK)
            src = gate_raw.rearrange("p k (d r) -> p (k d) r", r=RANK).unsqueeze(2)
            return ((v[:, 0:2 * KT], src.to_broadcast([P, 2 * KT, 2, RANK])),
                    (v[:, 2 * KT:], src[:, 0:2].to_broadcast([P, 2, 2, RANK])))

        def kv_banks(h):
            pair = ((GLA_AT[h] + 8) // 8 + 1) % 2
            return 2 * pair, 2 * pair + 1

        def tok_cols(buf, col):
            return (proj if buf == "proj" else kvm)[:, :, col:col + CH]

        def groups(ap, w):
            return ap.rearrange("p t (g w) -> p t g w", w=w)

        def silu_of_gate(act):
            for t in range(NT):
                last = act.activation(silu_g[:, t, :], ps[:, t, :], ACT.Silu, scale=rstd_h[:, t:t + 1])
            last.then_inc(gate_read, 1)

        def hidden_hi(act):
            act.activation(B_hi[:, 0:4, :].rearrange("p k t -> p (k t)"), ps[:, 6:8, :].rearrange("p b n -> p (b n)"),
                           ACT.Copy).then_inc(hT_hi, 1)

        def scale_groups(dve, i, ap, width):
            dve.wait_ge(n_rstd, i + 1)
            n = CH // width
            g = groups(ap, width)
            r = rstd_n[i][:, 0:NT * n].rearrange("p (t g) -> p t g", t=NT).unsqueeze(3)
            dve.tensor_tensor(g, g, r.to_broadcast([P, NT, n, width]), ALU.mult).then_inc(n_scaled, 1)

        @block.sync
        def _(sp):
            def load_x(c):
                sp.dma_start(xin[:, :, c * CH:(c + 1) * CH], x.rearrange("(t p) n -> p t n", p=P)[:, :, c * CH:(c + 1) * CH]
                             ).then_inc(x_landed[c], 16)

            load_x(0)

            def load(n, src, slot=None):
                s = n % RAW_SLOTS if slot is None else slot
                sp.dma_start(raw[:, s], src).then_inc(raw_landed[s], 16)

            def free(n):
                if n >= RAW_SLOTS:
                    sp.wait_ge(lo_ready, 2 * (n - RAW_SLOTS) + 2)

            n = 0
            for m, wcol, _, _ in CHUNKS:
                for k in range(4):
                    free(n)
                    load(n, rows(wkv if m else w_in, 4 * P * k, wcol))
                    if n == 0:
                        load_x(1)
                        load_x(2)
                    if n == 1:
                        load_x(3)
                        sp.dma_start(gate_raw, w_in[:, WG:WG + 2 * RANK].rearrange("(k p) c -> p k c", p=P)
                                     ).then_inc(gate_landed, 16)
                        for d, w in enumerate((wg2_f, wg2_b)):
                            sp.dma_start(wg2[:, d, :], w).then_inc(wg2_landed, 16)
                    n += 1
            for c, k in OUT_PIECES:
                free(n)
                load(n, rows(w_out, k * P, c * CH))
                n += 1
            for base in (0, DFF):
                for k in range(4):
                    free(n)
                    load(n, rows(w13, 4 * P * k, base))
                    n += 1
            with sp.Fori(1, FC) as i:
                for j in range(BODY // 2):
                    sp.wait_ge(lo_ready, i * BODY + (U_BODY - BODY + 2 * (j - RAW_SLOTS) + 2))
                    if j < 4:
                        src = rows(w13, 4 * P * j, i * CH)
                    elif j < 8:
                        src = rows(w2, i * CH - CH, (j - 4) * CH)
                    else:
                        src = rows(w13, 4 * P * (j - 8), i * CH + DFF)
                    load(0, src, slot=(U_BODY // 2 + j) % RAW_SLOTS)
            for c in range(4):
                n = U_TAIL // 2 + c
                free(n)
                load(n, rows(w2, (FC - 1) * CH, c * CH))
            for c in range(4):
                sp.wait_ge(col_added, 4 * FC + c + 1)
                sp.dma_start(out.rearrange("(t p) n -> p t n", p=P)[:, :, c * CH:(c + 1) * CH],
                             xin[:, :, c * CH:(c + 1) * CH]).then_inc(out_stored, 16)
            sp.wait_ge(out_stored, 64)

        @block.gpsimd
        def _(pool):
            link = linker(pool, pool_step)
            link(pool.memset(ident[:], 0.0))
            pool.affine_select(out=ident[:], in_=ident[:], compare_op=ALU.not_equal, fill=1.0, base=0,
                               pattern=[[-1, P]], channel_multiplier=1).then_inc(ident_ready, 1)
            pool.dma_start(rpb_sb[:], rpb.rearrange("h d c -> (h d) c")).then_inc(rpb_landed, 16)
            link(pool.memset(resets[:], 1.0))
            link(pool.memset(masks[:].bitcast(F32), 0.0))
            link(pool.memset(scoresT[:], 0.0))
            link(pool.memset(colmask[:], 0.0))
            link(pool.memset(pad, 0.0))
            link(pool.memset(resets[:, 0, :].rearrange("p (n c) -> p n c", c=GC)[:, :, 0:1], 0.0))
            link(pool.memset(resets[:, 1, :].rearrange("p (n c) -> p n c", c=GC)[:, :, GC - 1:GC], 0.0))
            ones = masks[:].bitcast(F32)
            for c in range(2):
                s = slice(c * GC, (c + 1) * GC)
                blk = ones[s, :, :, s]
                link(pool.memset(blk, 1.0))
                link(pool.affine_select(out=blk[:, 0], in_=blk[:, 0], compare_op=ALU.is_ge, fill=0.0, base=0,
                                        pattern=[[0, NT], [1, GC]], channel_multiplier=-1))
                link(pool.affine_select(out=blk[:, 1], in_=blk[:, 1], compare_op=ALU.is_gt, fill=0.0, base=0,
                                        pattern=[[0, NT], [-1, GC]], channel_multiplier=1))
                lowm, highm = colmask[s, 0:GW - WIN], colmask[s, WIN:GW]
                link(pool.affine_select(out=lowm, in_=lowm, compare_op=ALU.is_ge, fill=MASKED, base=WIN // 2,
                                        pattern=[[1, GW - WIN]], channel_multiplier=-1))
                link(pool.affine_select(out=highm, in_=highm, compare_op=ALU.is_ge, fill=MASKED,
                                        base=WIN // 2 - 1 - WIN, pattern=[[-1, GW - WIN]], channel_multiplier=1))
            pool.memset(half[:], -0.5).then_inc(masks_ready, 1)
            pool.wait_ge(rpb_landed, 16)
            pool.tensor_copy(pad[:, 48:48 + RB_C], rpb_sb[:, ::-1]).then_inc(pad_ready, 1)
            pool.wait_ge(pad_ready, 1)
            pool.dma_start(bias_rows[:].rearrange("h d c -> (h d) c"), pad).then_inc(rows_stored, 16)

            def inv_rms(src, dst, width, ready):
                link(pool.tensor_scalar(dst, src, 1.0 / width, EPS, ALU.mult, ALU.add))
                pool.tensor_tensor(dst, dst, half[:, 0:dst.shape[-1]], ALU.pow).then_inc(ready, 1)

            pool.wait_ge(x_squared, 2)
            inv_rms(ssq_x, rstd_x, D, rstd_x_ready)
            pool.wait_ge(m_squared, 2)
            inv_rms(ssq_m, rstd_m, D, rstd_m_ready)

            def norm(i, width):
                n = 2 * CH // width
                pool.wait_ge(n_summed, i + 1)
                inv_rms(ssq_n[i][:, 0:n], rstd_n[i][:, 0:n], width, n_rstd)

            pool.wait_ge(rows_stored, 16)

            def fetch_bias(h):
                for t in range(NT):
                    for r in range(2):
                        dr = RB_R // 2 - (2 * t + r)
                        src = bass.AP(tensor=bias_rows[:].tensor, offset=(h * RB_R + dr) * PADC,
                                      ap=[[1, GC], [PADC, NROW], [1, GW]])
                        pool.dma_start(bias_rev[h % 2][r * GC:(r + 1) * GC, t * NROW:(t + 1) * NROW, :],
                                       src).then_inc(rev_landed[h % 2], 16)

            def make_bias(h):
                pool.wait_ge(rev_landed[h % 2], 64 * (h // 2 + 1))
                if h >= 2:
                    pool.wait_ge(a_copied, h - 1)
                pool.tensor_tensor(bias[h % 2].rearrange("p t (a c) -> p (t a) c", c=GW), bias_rev[h % 2][:, :, ::-1],
                                   colmask[:].unsqueeze(1).to_broadcast([P, NT * NROW, GW]),
                                   ALU.add).then_inc(bias_ready, 1)

            norm(0, ND)
            norm(1, ND)
            pool.wait_ge(gates_done, 1)
            fetch_bias(0)
            fetch_bias(1)
            pool.wait_ge(g_z, GH)
            make_bias(0)
            make_bias(1)
            norm(2, MD)
            for h in range(2, NH):
                pool.wait_ge(bias_ready, h - 1)
                fetch_bias(h)
                make_bias(h)
                if h == 6:
                    norm(3, MD)
            pool.wait_ge(g_oevac, GH)
            inv_rms(ssq_o, rstd_o, GV, rstd_o_ready)
            norm(4, ND)
            norm(5, MD)
            pool.wait_ge(sum_h_ready, 1)
            inv_rms(sum_h, rstd_h, D, rstd_h_ready)

        @block.scalar
        def _(act):
            link = linker(act, act_step)
            for row, v in ((V_ATTN, attn_norm), (V_MEM, mem_norm), (V_FFN, ffn_norm), (V_OUT, gla_out),
                           (V_OUT + 8, na_out), (V_OUT + 12, mem_out), (V_BGF, bg_f), (V_BGB, bg_b),
                           (V_MQ, mem_q), (V_MK, mem_k)):
                n = v.shape[1] // P
                act.dma_start(vrow[row:row + n, :], v.rearrange("a (k p) -> (a k) p", p=P)
                              ).then_inc(gain_landed if row == V_ATTN else vec_landed, 16)
            for row, v in ((V_NQ, na_q), (V_NK, na_k)):
                for j in range(2):
                    act.dma_start(vrow[row:row + 1, j * ND:(j + 1) * ND], v).then_inc(vec_landed, 16)

            def split(u, wait_piece=True):
                if u % 2 == 0:
                    n = u // 2
                    act.wait_ge(raw_landed[n % RAW_SLOTS], 16 * (n // RAW_SLOTS + 1))
                if u >= UNIT_SLOTS:
                    act.wait_ge(unit_done, u - UNIT_SLOTS + 1)
                act.activation(w_hi[:, u % UNIT_SLOTS], raw[:, u // 2 % RAW_SLOTS, 2 * (u % 2):2 * (u % 2) + 2],
                               ACT.Copy).then_inc(hi_ready, 1)

            def evac_hi(dst, bank, k0, gains, n, done):
                for k in range(n):
                    last = act.activation(dst[:, k0 + k, :], ps[:, bank + k // 2, (k % 2) * T:(k % 2 + 1) * T],
                                          ACT.Copy, scale=vcol[:, gains + k:gains + k + 1])
                last.then_inc(done, 1)

            def evac_chunk(c):
                m, _, buf, col = CHUNKS[c]
                act.wait_ge(unit_done, 8 * c + 8)
                act.wait_ge(*((rstd_m_ready, 1) if m else (rstd_x_ready, 1)))
                dst, r = tok_cols(buf, col), (rstd_m if m else rstd_x)
                if c == 9:
                    act.wait_ge(n_summed, 4)
                if c >= 10:
                    act.wait_ge(a_copied, NH)
                func = ACT.Silu if c >= 10 else ACT.Copy
                for t in range(NT):
                    last = act.activation(dst[:, t, :], acc(c % 2)[:, t, :], func, scale=r[:, t:t + 1])
                last.then_inc(chunk_evac, 1)

            act.wait_ge(vcol_ready, 1)
            for u in range(U_BODY):
                if u < 8:
                    act.wait_ge(xT, u + 1)
                    evac_hi(A_hi, u, 2 * u, V_ATTN + 2 * u, 2, xT_hi)
                split(u)
                if u == 3:
                    act.wait_ge(gate_landed, 16)
                    for dst, src in gate_tiles(gate_hi):
                        last = act.activation(dst, src, ACT.Copy)
                    last.then_inc(gate_hi_ready, 1)
                if u in (8, 9):
                    t = u - 8
                    act.activation(row_scratch, xin[:, t, :], ACT.Square,
                                   accum_out=ssq_x[:, t:t + 1]).then_inc(x_squared, 1)
                    act.wait_ge(x_squared, t + 1)
                    if t == 1:
                        act.wait_ge(xT, 8)
                        act.dma_start(xin[:], mem.rearrange("(t p) n -> p t n", p=P)).then_inc(mem_landed, 16)
                if u % 8 == 3 and 11 <= u <= 99:
                    evac_chunk((u - 11) // 8)
                if u == 11:
                    act.wait_ge(gates_done, 1)
                    act.activation(gates_raw, ps[0:4 * RANK, 7, 0:T], ACT.Copy).then_inc(gates_evac, 1)
                if 17 <= u < 25:
                    b = u - 17
                    act.wait_ge(vcol_ready, 2)
                    act.wait_ge(mT, b + 1)
                    evac_hi(B_hi, MEM_BANKS[b % 3], 2 * b, V_MEM + 2 * b, 2, mT_hi)
                if u in (25, 26):
                    t = u - 25
                    act.activation(row_scratch, xin[:, t, :], ACT.Square,
                                   accum_out=ssq_m[:, t:t + 1]).then_inc(m_squared, 1)
                    act.wait_ge(m_squared, t + 1)
                    if t == 1:
                        act.wait_ge(mT, 8)
                        act.dma_start(xin[:], x.rearrange("(t p) n -> p t n", p=P)).then_inc(x_again, 16)
                for h, at in enumerate(GLA_AT):
                    if u == at + 4:
                        act.wait_ge(g_z, h + 1)
                        if h:
                            act.wait_ge(g_cum, h)
                        for d, b in enumerate((V_BGF, V_BGB)):
                            last = act.activation(softp[:, d, :], ps[:, 5, d * T:(d + 1) * T], ACT.Abs,
                                                  bias=vcol[:, b + h:b + h + 1])
                        last.then_inc(g_abs, 1)
                        act.wait_ge(g_abs, h + 1)
                        link(act.activation(softp[:], softp[:], ACT.Exp, scale=-1.0))
                        act.activation(softp[:], softp[:], ACT.Ln, bias=1.0).then_inc(g_soft, 1)
                    if u == at + 6:
                        act.wait_ge(g_cum, h + 1)
                        if h:
                            act.wait_ge(g_state, h)
                        act.activation(e_pos[:], cum[:], ACT.Exp, scale=1.0 / TAU)
                        act.activation(e_neg[:], cum[:], ACT.Exp, scale=-1.0 / TAU).then_inc(g_exp, 1)
                    if u == at + 10:
                        act.wait_ge(g_kendT, h + 1)
                        act.activation(k_tok[:].rearrange("p d t k -> p (d t k)"), ps[:, 7, :],
                                       ACT.Copy).then_inc(g_ktok, 1)
                    if u == at + 14:
                        act.wait_ge(g_o, h + 1)
                        act.activation(proj[:, :, PV + h * GV:PV + (h + 1) * GV],
                                       ps[:, 6, :].rearrange("p (t v) -> p t v", t=NT), ACT.Copy)
                        for t in range(NT):
                            last = act.activation(k_tok[:, t].rearrange("p t k -> p (t k)"),
                                                  ps[:, 6, t * GV:(t + 1) * GV], ACT.Square,
                                                  accum_out=ssq_o[:, 2 * h + t:2 * h + t + 1])
                        last.then_inc(g_oevac, 1)
                for i, (buf, col, width, at, _) in enumerate(NORMS):
                    if u == at:
                        act.wait_ge(chunk_evac, {NQ: 5, NK: 6, 0: 7, MQ: 9}[col])
                        if i:
                            act.wait_ge(n_summed, i)
                        act.activation(psq, tok_cols(buf, col), ACT.Square).then_inc(n_squared, 1)
                for i, (col, width, at, _) in enumerate(ONORMS):
                    if u == at:
                        act.wait_ge(a_out, i + 1)
                        act.wait_ge(a_scored, NH)
                        if i:
                            act.wait_ge(n_summed, 5)
                        act.activation(osq[:], tok_cols("proj", col), ACT.Square).then_inc(n_squared, 1)
                for i, (at, dst, bank, gain) in enumerate(((61, na_qT, 4, V_NQ), (66, na_kT, 6, V_NK),
                                                           (71, mem_kT, 2, V_MK), (81, mem_qT, 0, V_MQ))):
                    if u == at:
                        act.wait_ge(headT, i + 1)
                        act.activation(dst[:, 0:2, :].rearrange("p j t -> p (j t)"), ps[:, bank, :], ACT.Copy,
                                       scale=vcol[:, gain:gain + 1]).then_inc(headT_evac, 1)
                for g, at in enumerate(ATT_AT):
                    if u == at + 5:
                        act.wait_ge(a_max, g + 1)
                        if g >= 2:
                            act.wait_ge(a_pT, g - 1)
                        for t in range(NT):
                            ins = act.activation(probs[:, g % 2, t, :], scores[:, g % 2, t, :], ACT.Exp,
                                                 bias=negmax[:, g % 2, t:t + 1], accum_out=psum_e[:, g, t:t + 1])
                            if t == 1:
                                ins.then_inc(a_exp, 1)
                    if u == at + 8:
                        act.wait_ge(a_pT, g + 1)
                        if g >= 2:
                            act.wait_ge(a_pv, g - 1)
                        act.activation(probsT[:, g % 2].rearrange("p k q -> p (k q)"), ps[:, 5, :],
                                       ACT.Copy).then_inc(a_pTevac, 1)
                for i, (at, k0, bank) in enumerate(((94, 0, 0), (97, 8, 0), (103, 4, 4), (105, 12, 6))):
                    if u == at:
                        act.wait_ge(yT, i + 1)
                        evac_hi(B_hi, bank, k0, V_OUT + k0, 4, yT_hi)
                for c, (at, _, at2) in enumerate(X1_AT):
                    if u == at + 1:
                        act.wait_ge(col_added, c + 1)
                        if c:
                            act.wait_ge(x1_squared, c)
                        for t in range(NT):
                            last = act.activation(silu_g[:, t, :], xin[:, t, c * CH:(c + 1) * CH], ACT.Square,
                                                  accum_out=ssq_h[:, 4 * t + c:4 * t + c + 1])
                        last.then_inc(x1_squared, 1)
                    if u == at2:
                        act.wait_ge(x1T, c + 1)
                        evac_hi(A_hi, 4, 4 * c, V_FFN + 4 * c, 4, x1T_hi)
                if u == U_FFN + 11:
                    act.wait_ge(unit_done, U_FFN + 8)
                    act.wait_ge(rstd_h_ready, 1)
                    silu_of_gate(act)

            with act.Fori(1, FC) as i:
                for j in range(BODY):
                    if j % 2 == 0:
                        n = U_BODY // 2 + j // 2
                        act.wait_ge(raw_landed[n % RAW_SLOTS],
                                    i * (16 * BODY // 2 // RAW_SLOTS)
                                    + (16 * (n // RAW_SLOTS + 1) - 16 * BODY // 2 // RAW_SLOTS))
                    act.wait_ge(unit_done, i * BODY + (U_BODY - BODY + j - UNIT_SLOTS + 1))
                    act.activation(w_hi[:, (U_BODY + j) % UNIT_SLOTS],
                                   raw[:, (U_BODY + j) // 2 % RAW_SLOTS, 2 * (j % 2):2 * (j % 2) + 2],
                                   ACT.Copy).then_inc(hi_ready, 1)
                    if j == 6:
                        act.wait_ge(hT, i)
                        hidden_hi(act)
                    if j == 11:
                        act.wait_ge(unit_done, i * BODY + (U_BODY - BODY + 8))
                        act.wait_ge(h_ready, i)
                        silu_of_gate(act)
            for u in range(U_TAIL, U_TAIL + 8):
                if u == U_TAIL + 3:
                    act.wait_ge(hT, FC)
                    hidden_hi(act)
                split(u)

        @block.vector
        def _(dve):
            link = linker(dve, dve_step)

            def split(u):
                dve.wait_ge(hi_ready, u + 1)
                dve.tensor_tensor(w_lo[:, u % UNIT_SLOTS], raw[:, u // 2 % RAW_SLOTS, 2 * (u % 2):2 * (u % 2) + 2],
                                  w_hi[:, u % UNIT_SLOTS].bitcast(F32), ALU.subtract).then_inc(lo_ready, 1)

            def evac_lo(dst, high, bank, k0, gains, n, done):
                for k in range(n):
                    last = dve.scalar_tensor_tensor(dst[:, k0 + k, :], ps[:, bank + k // 2, (k % 2) * T:(k % 2 + 1) * T],
                                                    vcol[:, gains + k:gains + k + 1],
                                                    high[:, k0 + k, :].bitcast(F32), ALU.mult, ALU.subtract)
                last.then_inc(done, 1)

            dve.wait_ge(vecT, 1)
            dve.tensor_copy(vcol[:, 0:KT], ps[:, 7, 0:KT]).then_inc(vcol_ready, 1)
            for u in range(U_BODY):
                if u < 8:
                    dve.wait_ge(xT_hi, u + 1)
                    if u == 0:
                        dve.wait_ge(vcol_ready, 1)
                    evac_lo(A_lo, A_hi, u, 2 * u, V_ATTN + 2 * u, 2, xT_lo)
                split(u)
                if u == 4:
                    dve.wait_ge(gate_hi_ready, 1)
                    for (dst, src), (high, _) in zip(gate_tiles(gate_lo), gate_tiles(gate_hi)):
                        last = dve.tensor_tensor(dst, src, high.bitcast(F32), ALU.subtract)
                    last.then_inc(gate_lo_ready, 1)
                if u == 7:
                    dve.wait_ge(vecT, 2)
                    dve.tensor_copy(vcol[:, KT:V_ROWS], ps[:, 2, KT:V_ROWS]).then_inc(vcol_ready, 1)
                if u == 15:
                    dve.wait_ge(gates_evac, 1)
                    dve.wait_ge(rstd_rows, 1)
                    for d in range(2):
                        r = slice(2 * RANK * d, 2 * RANK * d + RANK)
                        last = dve.tensor_tensor(gT[:, d, :], gates_raw[r], ps[r, 4, 0:T], ALU.mult)
                    last.then_inc(gT_ready, 1)
                if 17 <= u < 25:
                    b = u - 17
                    dve.wait_ge(mT_hi, b + 1)
                    evac_lo(B_lo, B_hi, MEM_BANKS[b % 3], 2 * b, V_MEM + 2 * b, 2, mT_lo)
                for h, at in enumerate(GLA_AT):
                    if u == at + 4:
                        if h == 0:
                            dve.wait_ge(masks_ready, 1)
                        dve.wait_ge(g_abs, h + 1)
                        for d, b in enumerate((V_BGF, V_BGB)):
                            link(dve.tensor_scalar(la[:, d, :], ps[:, 5, d * T:(d + 1) * T],
                                                   vcol[:, b + h:b + h + 1], 0.0, ALU.add, ALU.min))
                    if u == at + 5:
                        dve.wait_ge(g_soft, h + 1)
                        link(dve.tensor_tensor(la[:], la[:], softp[:], ALU.subtract))
                        if h:
                            dve.wait_ge(g_exp, h)
                        for d, step in ((0, 1), (1, -1)):
                            for t in range(NT):
                                s = slice(t * P, (t + 1) * P)
                                last = dve.tensor_tensor_scan(cum[:, d, s][:, ::step], resets[:, d, :][:, ::step],
                                                              la[:, d, s][:, ::step], 0.0, ALU.mult, ALU.add)
                        last.then_inc(g_cum, 1)
                    if u == at + 7:
                        dve.wait_ge(g_exp, h + 1)
                        dve.wait_ge(g_qkT, h + 1)
                        if h:
                            dve.wait_ge(g_o, h)
                        for d in range(2):
                            dve.scalar_tensor_tensor(q_e[:, d, :], ps[:, 4, 0:T], GK ** -0.5, e_pos[:, d, :],
                                                     ALU.mult, ALU.mult)
                            link(dve.tensor_tensor(k_e[:, d, :], ps[:, 4, T:2 * T], e_neg[:, d, :], ALU.mult))
                        for d, edge in enumerate((GC - 1, 0)):
                            ch = lambda ap: ap.rearrange("p (n c) -> p n c", c=GC)
                            last = dve.tensor_tensor(ch(k_end[:, d, :]), ch(k_e[:, d, :]),
                                                     ch(e_pos[:, d, :])[:, :, edge:edge + 1].to_broadcast([P, NCH, GC]),
                                                     ALU.mult)
                        last.then_inc(g_gated, 1)
                    if u == at + 10:
                        dve.wait_ge(g_scores, h + 1)
                        for d in range(2):
                            ins = dve.copy_predicated(scoresT[:].rearrange("p t q -> p (t q)"),
                                                      masks[:, d].rearrange("p t q -> p (t q)"),
                                                      ps[:, 6, d * T:(d + 1) * T])
                            if d == 0:
                                link(ins)
                        ins.then_inc(g_masked, 1)
                    if u == at + 12:
                        dve.wait_ge(g_kv, h + 1)
                        f, b = kv_banks(h)
                        dve.tensor_copy(states[:, 0, 0, :], ps[:, f, 0:GV])
                        link(dve.tensor_copy(states[:, 1, 0, :], ps[:, b, GV:2 * GV]))
                        dve.scalar_tensor_tensor(states[:, 0, 1, :], states[:, 0, 0, :],
                                                 e_pos[:, 0, 2 * GC - 1:2 * GC], ps[:, b, 0:GV], ALU.mult, ALU.add)
                        link(dve.scalar_tensor_tensor(states[:, 1, 1, :], states[:, 1, 0, :],
                                                      e_pos[:, 1, 2 * GC:2 * GC + 1], ps[:, 7, 0:GV],
                                                      ALU.mult, ALU.add))
                        dve.scalar_tensor_tensor(states[:, 0, 2, :], states[:, 0, 1, :],
                                                 e_pos[:, 0, 3 * GC - 1:3 * GC], ps[:, f, GV:2 * GV], ALU.mult, ALU.add)
                        dve.wait_ge(g_kvx, h + 1)
                        dve.scalar_tensor_tensor(states[:, 1, 2, :], states[:, 1, 1, :],
                                                 e_pos[:, 1, GC:GC + 1], ps[:, 6, 0:GV],
                                                 ALU.mult, ALU.add).then_inc(g_state, 1)
                for i, (buf, col, width, at, at2) in enumerate(NORMS):
                    if u == at + 1:
                        dve.wait_ge(n_squared, i + 1)
                        dve.tensor_reduce(ssq_n[i][:, 0:2 * CH // width].rearrange("p (t g) -> p t g", t=NT),
                                          groups(psq, width), AX, ALU.add).then_inc(n_summed, 1)
                    if u == at2:
                        scale_groups(dve, i, tok_cols(buf, col), width)
                for i, (col, width, at, at2) in enumerate(ONORMS):
                    if u == at + 1:
                        dve.wait_ge(n_squared, 5 + i)
                        dve.tensor_reduce(ssq_n[4 + i][:, 0:2 * CH // width].rearrange("p (t g) -> p t g", t=NT),
                                          groups(osq[:], width), AX, ALU.add).then_inc(n_summed, 1)
                    if u == at2:
                        scale_groups(dve, 4 + i, tok_cols("proj", col), width)
                for i, (at, dst, bank, gain) in enumerate(((61, na_qT, 4, V_NQ), (66, na_kT, 6, V_NK),
                                                           (71, mem_kT, 2, V_MK), (81, mem_qT, 0, V_MQ))):
                    if u == at:
                        dve.wait_ge(headT, i + 1)
                        dve.tensor_scalar(dst[:, 2:4, :].rearrange("p j t -> p (j t)"), ps[:, bank + 1, :],
                                          vcol[:, gain:gain + 1], None, ALU.mult).then_inc(headT_evac, 1)
                for g, at in enumerate(ATT_AT):
                    if u == at + 4:
                        dve.wait_ge(a_scored, g + 1)
                        if g >= 2:
                            dve.wait_ge(a_exp, g - 1)
                        sc = ps[:, 4, :].rearrange("p (t k) -> p t k", t=NT)
                        if g < NH:
                            dve.wait_ge(bias_ready, g + 1)
                            dve.scalar_tensor_tensor(scores[:, g % 2], sc, ND ** -0.5, bias[g % 2],
                                                     ALU.mult, ALU.add).then_inc(a_copied, 1)
                        else:
                            dve.tensor_scalar(scores[:, g % 2], sc, MD ** -0.5, None, ALU.mult).then_inc(a_copied, 1)
                        dve.wait_ge(a_copied, g + 1)
                        dve.tensor_reduce(negmax[:, g % 2, :], scores[:, g % 2], AX, ALU.max,
                                          negate=True).then_inc(a_max, 1)
                for i, (at, g0, ng, w, col) in enumerate(((90, 0, NH, ND, NQ), (99, NH, MH, MD, MQ))):
                    if u == at:
                        dve.wait_ge(a_pv, g0 + ng)
                        dve.wait_ge(a_exp, g0 + ng)
                        if i == 1:
                            dve.wait_ge(headT, 4)
                        link(dve.reciprocal(rinv[:, g0:g0 + ng, :], psum_e[:, g0:g0 + ng, :]))
                        for t in range(NT):
                            last = dve.tensor_tensor(groups(tok_cols("proj", col), w)[:, t],
                                                     ps[:, 6 + t, :].rearrange("p (g w) -> p g w", w=w),
                                                     rinv[:, g0:g0 + ng, t:t + 1].to_broadcast([P, ng, w]), ALU.mult)
                        last.then_inc(a_out, 1)
                for at, c in ((92, 0), (100, 1)):
                    if u == at:
                        dve.wait_ge(chunk_evac, 11 + c)
                        dve.wait_ge(rstd_o_ready, 1)
                        for h in (2 * c, 2 * c + 1):
                            for t in range(NT):
                                o = proj[:, t, PV + h * GV:PV + (h + 1) * GV]
                                last = dve.scalar_tensor_tensor(o, o, rstd_o[:, 2 * h + t:2 * h + t + 1],
                                                                proj[:, t, PR + h * GV:PR + (h + 1) * GV],
                                                                ALU.mult, ALU.mult)
                        last.then_inc(y_ready, 1)
                for i, (at, k0, bank) in enumerate(((94, 0, 0), (97, 8, 0), (103, 4, 4), (105, 12, 6))):
                    if u == at:
                        dve.wait_ge(yT_hi, i + 1)
                        evac_lo(B_lo, B_hi, bank, k0, V_OUT + k0, 4, yT_lo)
                for c, (at, _, at2) in enumerate(X1_AT):
                    if u == at:
                        dve.wait_ge(unit_done, U_OUT + (12, 16, 24, 32)[c])
                        dve.wait_ge(x_again, 16)
                        xc = xin[:, :, c * CH:(c + 1) * CH]
                        dve.tensor_tensor(xc, acc(c % 2), xc, ALU.add).then_inc(col_added, 1)
                    if u == at2:
                        dve.wait_ge(x1T_hi, c + 1)
                        evac_lo(A_lo, A_hi, 4, 4 * c, V_FFN + 4 * c, 4, x1T_lo)
                if u == 134:
                    dve.wait_ge(x1_squared, 4)
                    dve.tensor_reduce(sum_h, ssq_h.rearrange("p (t c) -> p t c", t=NT), AX, ALU.add
                                      ).then_inc(sum_h_ready, 1)

            def gate_times_up():
                for t in range(NT):
                    last = dve.scalar_tensor_tensor(h_tok[:, t, :], ps[:, 2 + t, :], rstd_h[:, t:t + 1],
                                                    silu_g[:, t, :], ALU.mult, ALU.mult)
                last.then_inc(h_ready, 1)

            def hidden_lo():
                dve.tensor_tensor(B_lo[:, 0:4, :].rearrange("p k t -> p (k t)"),
                                  ps[:, 6:8, :].rearrange("p b n -> p (b n)"),
                                  B_hi[:, 0:4, :].rearrange("p k t -> p (k t)").bitcast(F32),
                                  ALU.subtract).then_inc(hT_lo, 1)

            def add_down(c, bank):
                xc = xin[:, :, c * CH:(c + 1) * CH]
                dve.tensor_tensor(xc, ps[:, bank:bank + 2, :], xc, ALU.add).then_inc(col_added, 1)

            with dve.Fori(1, FC) as i:
                for j in range(BODY):
                    dve.wait_ge(hi_ready, i * BODY + (U_BODY - BODY + j + 1))
                    dve.tensor_tensor(w_lo[:, (U_BODY + j) % UNIT_SLOTS],
                                      raw[:, (U_BODY + j) // 2 % RAW_SLOTS, 2 * (j % 2):2 * (j % 2) + 2],
                                      w_hi[:, (U_BODY + j) % UNIT_SLOTS].bitcast(F32),
                                      ALU.subtract).then_inc(lo_ready, 1)
                    if j == 3:
                        dve.wait_ge(unit_done, i * BODY + (U_BODY - BODY))
                        dve.wait_ge(gate_read, i)
                        gate_times_up()
                    if j == 6:
                        dve.wait_ge(hT_hi, i)
                        hidden_lo()
                    if j in (13, 15, 17, 19):
                        c = (j - 13) // 2
                        dve.wait_ge(unit_done, i * BODY + (U_BODY - BODY + 10 + 2 * c))
                        if j == 13:
                            dve.wait_ge(x1_squared, 4)
                        dve.wait_ge(col_added, i * 4 + c)
                        add_down(c, DOWN_BANKS[c])
            for u in range(U_TAIL, U_TAIL + 8):
                split(u)
                if u == U_TAIL:
                    dve.wait_ge(unit_done, U_TAIL)
                    dve.wait_ge(gate_read, FC)
                    gate_times_up()
                if u == U_TAIL + 2:
                    dve.wait_ge(hT_hi, FC)
                    hidden_lo()
                if u == U_TAIL + 6:
                    dve.wait_ge(unit_done, U_TAIL + 2)
                    dve.wait_ge(col_added, 4 * FC)
                    add_down(0, 4)
            for c in range(1, 4):
                dve.wait_ge(unit_done, U_TAIL + 2 * c + 2)
                add_down(c, DOWN_BANKS[c])

        @block.tensor
        def _(pe):
            def unit(hi, lo, k0, bank, s, first, last):
                for k in range(2):
                    for t in range(NT):
                        tok = slice(t * P, (t + 1) * P)
                        for n, (a, w) in enumerate(((hi, w_hi), (hi, w_lo), (lo, w_hi))):
                            mm = pe.matmul(ps[:, bank + t, :], a[:, k0 + k, tok], w[:, s, k, :],
                                           start=first and k == 0 and n == 0, stop=last and k == 1 and n == 2)
                mm.then_inc(unit_done, 1)

            def transposes(src_of, bank, n, done):
                for j in range(n):
                    for t in range(NT):
                        at = (j % 2) * T + t * P
                        last = pe.transpose(ps[:, bank + j // 2, at:at + P], src_of(j, t), ident[:])
                last.then_inc(done, 1)

            pe.wait_ge(ident_ready, 1)
            pe.wait_ge(gain_landed, 16)
            pe.transpose(ps[:, 7, 0:KT], vrow[0:KT, :], ident[0:KT, 0:KT]).then_inc(vecT, 1)
            for b in range(8):
                pe.wait_ge(x_landed[b // 2], 16)
                if b == 7:
                    pe.wait_ge(vcol_ready, 1)
                transposes(lambda j, t: xin[:, t, (2 * b + j) * P:(2 * b + j + 1) * P], b, 2, xT)

            for u in range(U_BODY):
                pe.wait_ge(lo_ready, u + 1)
                if u < U_OUT:
                    c, q = u // 8, u % 8
                    if u < 8:
                        pe.wait_ge(xT_lo, u + 1)
                    if q == 0:
                        if c == 1:
                            pe.wait_ge(vcol_ready, 2)
                        if 4 <= c < 4 + GH:
                            pe.wait_ge(g_state, c - 3)
                        if c >= 2:
                            pe.wait_ge(chunk_evac, c - 1)
                        if c == 6:
                            pe.wait_ge(mT_lo, 8)
                        if c == 9:
                            pe.wait_ge(headT_evac, 6)
                        if c == 10:
                            pe.wait_ge(headT_evac, 8)
                    if u == 0:
                        pe.wait_ge(xT_lo, 2)
                    m = CHUNKS[c][0]
                    unit(B_hi if m else A_hi, B_lo if m else A_lo, 2 * q, 2 * (c % 2), u % UNIT_SLOTS, q == 0, q == 7)
                elif u < U_FFN:
                    c, k0 = OUT_PIECES[(u - U_OUT) // 2]
                    k = k0 + 2 * (u % 2)
                    if u == U_OUT:
                        pe.wait_ge(yT_lo, 2)
                    if u == U_OUT + 4:
                        pe.wait_ge(chunk_evac, 12)
                    if u == U_OUT + 8:
                        pe.wait_ge(yT_lo, 4)
                    if u == U_OUT + 16:
                        pe.wait_ge(col_added, 1)
                    if u == U_OUT + 24:
                        pe.wait_ge(col_added, 2)
                    unit(B_hi, B_lo, k, 2 * (c % 2), u % UNIT_SLOTS, k == 8, k == 6)
                else:
                    q = (u - U_FFN) % 8
                    if u == U_FFN:
                        pe.wait_ge(col_added, 3)
                        pe.wait_ge(x1T_lo, 3)
                    if u == U_FFN + 6:
                        pe.wait_ge(x1T_lo, 4)
                    if u == U_FFN + 8:
                        pe.wait_ge(col_added, 4)
                    unit(A_hi, A_lo, 2 * q, 2 * ((u - U_FFN) // 8), u % UNIT_SLOTS, q == 0, q == 7)

                if u == 4:
                    pe.wait_ge(vec_landed, 16 * 13)
                    pe.wait_ge(xT_lo, 3)
                    pe.transpose(ps[:, 2, 0:V_ROWS], vrow[:], ident[0:V_ROWS, 0:V_ROWS]).then_inc(vecT, 1)
                if u == 7:
                    pe.wait_ge(gate_lo_ready, 1)
                    pe.wait_ge(xT_lo, 8)
                    for k in range(KT):
                        for n, (w, a) in enumerate(((gate_hi, A_hi), (gate_lo, A_hi), (gate_hi, A_lo))):
                            mm = pe.matmul(ps[:, 7, 0:T], w[:, 4 * RANK * k:4 * RANK * k + P], a[:, k, :],
                                           start=k == 0 and n == 0, stop=k == KT - 1 and n == 2)
                    mm.then_inc(gates_done, 1)
                if u == 11:
                    pe.wait_ge(rstd_x_ready, 1)
                    for t in range(NT):
                        last = pe.matmul(ps[:, 4, t * P:(t + 1) * P], rstd_x[:, t:t + 1].to_broadcast([P, P]), ident[:],
                                         start=True, stop=True)
                    last.then_inc(rstd_rows, 1)
                if 13 <= u < 21:
                    b = u - 13
                    if b == 0:
                        pe.wait_ge(mem_landed, 16)
                    if b >= 3:
                        pe.wait_ge(mT_lo, b - 2)
                    transposes(lambda j, t: xin[:, t, (2 * b + j) * P:(2 * b + j + 1) * P], MEM_BANKS[b % 3], 2, mT)
                for h, at in enumerate(GLA_AT):
                    if u == at:
                        pe.wait_ge(chunk_evac, 2)
                        pe.wait_ge(gT_ready, 1)
                        pe.wait_ge(mT_lo, 6)
                        if h:
                            pe.wait_ge(g_gated, h)
                        for j, col in enumerate((PQ, PK)):
                            for t in range(NT):
                                last = pe.transpose(ps[:, 4, j * T + t * P:j * T + (t + 1) * P],
                                                    proj[:, t, col + h * GK:col + (h + 1) * GK], ident[:])
                        last.then_inc(g_qkT, 1)
                        pe.wait_ge(wg2_landed, 32)
                        for d in range(2):
                            last = pe.matmul(ps[:, 5, d * T:(d + 1) * T], wg2[:, d, h * GK:(h + 1) * GK], gT[:, d, :],
                                             start=True, stop=True)
                        last.then_inc(g_z, 1)
                    if u == at + 7:
                        pe.wait_ge(g_gated, h + 1)
                        pe.wait_ge(mT_lo, 8)
                        if h:
                            pe.wait_ge(g_oevac, h)
                        for d in range(2):
                            for t in range(NT):
                                s = slice(t * P, (t + 1) * P)
                                last = pe.matmul(ps[:, 6, d * T + t * P:d * T + (t + 1) * P], k_e[:, d, s],
                                                 q_e[:, d, s], start=True, stop=True)
                        last.then_inc(g_scores, 1)
                        for d in range(2):
                            for t in range(NT):
                                at2 = (2 * d + t) * P
                                last = pe.transpose(ps[:, 7, at2:at2 + P], k_end[:, d, t * P:(t + 1) * P], ident[:])
                        last.then_inc(g_kendT, 1)
                    if u == at + 8:
                        pe.wait_ge(g_ktok, h + 1)
                        pe.wait_ge(chunk_evac, 3 + h)
                        f, b = kv_banks(h)
                        for d, n, bank, half_ in ((0, 0, f, 0), (0, 2, f, 1), (1, 2, 7, 0), (0, 1, b, 0), (1, 3, b, 1)):
                            r = slice((n % 2) * GC, (n % 2 + 1) * GC)
                            last = pe.matmul(ps[:, bank, half_ * GV:(half_ + 1) * GV], k_tok[r, d, n // 2, :],
                                             proj[r, n // 2, PV + h * GV:PV + (h + 1) * GV], start=True, stop=True)
                        last.then_inc(g_kv, 1)
                        pe.wait_ge(g_masked, h + 1)
                        pe.matmul(ps[:, 6, 0:GV], k_tok[GC:P, 1, 0, :], proj[GC:P, 0, PV + h * GV:PV + (h + 1) * GV],
                                  start=True, stop=True).then_inc(g_kvx, 1)
                    if u == at + 11:
                        pe.wait_ge(g_state, h + 1)
                        for t in range(NT):
                            o = ps[:, 6, t * GV:(t + 1) * GV]
                            terms = [(1, 0, 2), (0, 1, 0), (1, 1, 1)] if t == 0 else [(0, 2, 1), (1, 2, 0), (0, 3, 2)]
                            for k, (d, n, s) in enumerate(terms):
                                r = slice((n % 2) * GC, (n % 2 + 1) * GC)
                                pe.matmul(o[r, :], q_e[:, d, n * GC:(n + 1) * GC], states[:, d, s, :],
                                          start=k == 0 or terms[k - 1][1] != n, stop=False, skip_group_check=True)
                            last = pe.matmul(o, scoresT[:, t, :], proj[:, t, PV + h * GV:PV + (h + 1) * GV],
                                             start=False, stop=True, skip_group_check=True)
                        last.then_inc(g_o, 1)
                for i, (at, buf, col, bank, scaled) in enumerate(((57, "proj", NQ, 4, 1), (62, "proj", NK, 6, 2),
                                                                  (68, "kvm", 0, 2, 3), (78, "proj", MQ, 0, 4))):
                    if u == at:
                        pe.wait_ge(n_scaled, scaled)
                        if i == 0:
                            pe.wait_ge(g_state, GH)
                        if i == 1:
                            pe.wait_ge(g_oevac, GH)
                        if i == 2:
                            pe.wait_ge(chunk_evac, 8)
                        if i == 3:
                            pe.wait_ge(chunk_evac, 9)
                        transposes(lambda j, t: tok_cols(buf, col)[:, t, j * P:(j + 1) * P], bank, 4, headT)
                for g, at in enumerate(ATT_AT):
                    if u == at:
                        if g == 0:
                            pe.wait_ge(headT_evac, 4)
                        else:
                            pe.wait_ge(a_copied, g)
                        if g == NH:
                            pe.wait_ge(headT_evac, 8)
                        for t in range(NT):
                            q = slice(t * P, (t + 1) * P)
                            if g < NH:
                                r = slice((g % 2) * ND, (g % 2 + 1) * ND)
                                lhs, rhs = na_qT[r, g // 2, q], na_kT[r, g // 2, :]
                            else:
                                lhs, rhs = mem_qT[:, g - NH, q], mem_kT[:, g - NH, :]
                            last = pe.matmul(ps[:, 4, t * T:(t + 1) * T], lhs, rhs, start=True, stop=True)
                        last.then_inc(a_scored, 1)
                    if u == at + 4:
                        pe.wait_ge(a_exp, g + 1)
                        if g:
                            pe.wait_ge(a_pTevac, g)
                        for k in range(NT):
                            for t in range(NT):
                                last = pe.transpose(ps[:, 5, k * T + t * P:k * T + (t + 1) * P],
                                                    probs[:, g % 2, t, k * P:(k + 1) * P], ident[:])
                        last.then_inc(a_pT, 1)
                    if u == at + 7:
                        pe.wait_ge(a_pTevac, g + 1)
                        if g == 0:
                            pe.wait_ge(chunk_evac, 8)
                        if g == NH:
                            pe.wait_ge(chunk_evac, 10)
                            pe.wait_ge(a_out, 1)
                        w = ND if g < NH else MD
                        h = g if g < NH else g - NH
                        v = proj[:, :, NV:NV + CH] if g < NH else kvm[:, :, CH:2 * CH]
                        for t in range(NT):
                            for k in range(NT):
                                last = pe.matmul(ps[:, 6 + t, h * w:(h + 1) * w], probsT[:, g % 2, k, t * P:(t + 1) * P],
                                                 v[:, k, h * w:(h + 1) * w], start=k == 0, stop=k == NT - 1)
                        last.then_inc(a_pv, 1)
                for i, (at, col, bank) in enumerate(((91, PV, 0), (94, NQ, 0), (100, PV + CH, 4), (102, MQ, 6))):
                    if u == at:
                        if i == 0:
                            pe.wait_ge(y_ready, 1)
                            pe.wait_ge(chunk_evac, 11)
                        if i == 1:
                            pe.wait_ge(n_scaled, 5)
                            pe.wait_ge(yT_lo, 1)
                        if i == 2:
                            pe.wait_ge(y_ready, 2)
                        if i == 3:
                            pe.wait_ge(n_scaled, 6)
                        transposes(lambda j, t: proj[:, t, col + j * P:col + (j + 1) * P], bank, 4, yT)
                for c, (_, at, _) in enumerate(X1_AT):
                    if u == at:
                        pe.wait_ge(col_added, c + 1)
                        pe.wait_ge(x1T_lo, c) if c else pe.wait_ge(yT_lo, 3)
                        transposes(lambda j, t: xin[:, t, c * CH + j * P:c * CH + (j + 1) * P], 4, 4, x1T)

            with pe.Fori(1, FC) as i:
                for j in range(BODY):
                    pe.wait_ge(lo_ready, i * BODY + (U_BODY - BODY + j + 1))
                    s = (U_BODY + j) % UNIT_SLOTS
                    if j < 8:
                        if j == 0:
                            pe.wait_ge(gate_read, i)
                            pe.wait_ge(col_added, i * 4)
                        unit(A_hi, A_lo, 2 * j, 0, s, j == 0, j == 7)
                    elif j < 16:
                        c, k = (j - 8) // 2, 2 * (j % 2)
                        if j == 8:
                            pe.wait_ge(hT_lo, i)
                        if j == 10:
                            pe.wait_ge(gate_read, i + 1)
                        if j == 14:
                            pe.wait_ge(col_added, i * 4 + 1)
                        unit(B_hi, B_lo, k, DOWN_BANKS[c], s, k == 0, k == 2)
                    else:
                        if j == 16:
                            pe.wait_ge(h_ready, i)
                        unit(A_hi, A_lo, 2 * (j - 16), 2, s, j == 16, j == 23)
                    if j == 2:
                        pe.wait_ge(h_ready, i)
                        transposes(lambda j, t: h_tok[:, t, j * P:(j + 1) * P], 6, 4, hT)
            pe.wait_ge(h_ready, FC)
            transposes(lambda j, t: h_tok[:, t, j * P:(j + 1) * P], 6, 4, hT)
            for u in range(U_TAIL, U_TAIL + 8):
                c, k = (u - U_TAIL) // 2, 2 * (u % 2)
                pe.wait_ge(lo_ready, u + 1)
                if c == 0 and k == 0:
                    pe.wait_ge(hT_lo, FC)
                    pe.wait_ge(col_added, 4 * FC)
                if c == 3 and k == 0:
                    pe.wait_ge(col_added, 4 * FC + 1)
                unit(B_hi, B_lo, k, DOWN_BANKS[c], u % UNIT_SLOTS, k == 0, k == 2)


_INS = ["x", "mem", "attn_norm", "w_in", "gla_wg2_f", "gla_bg_f", "gla_wg2_b", "gla_bg_b", "gla_out_norm",
        "na_q_norm", "na_k_norm", "na_rpb", "na_out_norm", "mem_norm", "mem_wkv", "mem_q_norm", "mem_k_norm",
        "mem_out_norm", "w_out", "ffn_norm", "ffn_w13", "ffn_w2"]
_SQUEEZE = {"x", "mem", "w_in", "gla_wg2_f", "gla_wg2_b", "na_rpb", "mem_wkv", "w_out", "ffn_w13", "ffn_w2"}


def kernel(**inputs):
    import numpy as _np
    import concourse.bacc as _bacc
    from concourse import mybir as _mybir
    from concourse.bass_utils import run_bass_kernel_spmd as _run

    nc = _bacc.Bacc("TRN2", target_bir_lowering=False, num_devices=1)
    arrays, args = {}, []
    for name in _INS:
        a = _np.ascontiguousarray(inputs[name])
        if name in _SQUEEZE:
            a = a.reshape(a.shape[1:])
        arrays[f"in_{name}_dram"] = a
        args.append(nc.dram_tensor(f"in_{name}_dram", a.shape, _mybir.dt.from_np(a.dtype), kind="ExternalInput").ap())
    out = nc.dram_tensor("out_0_dram", (T, D), F32, kind="ExternalOutput").ap()
    build_layer(nc, *args, out)
    r = _run(nc, [arrays], core_ids=[0])
    return r.results[0]["out_0_dram"].reshape(1, T, D)
```

```python
from contextlib import ExitStack

import concourse.bass as bass
from concourse import mybir

F32 = mybir.dt.float32
F32R = mybir.dt.float32r
I32 = mybir.dt.int32
ALU = mybir.AluOpType
ACT = mybir.ActivationFunctionType
AX = mybir.AxisListType.X

P = 128
NT = 2
T = NT * P
D = 2048
KT = D // P
CH = 512
GH, GK, GV = 4, 128, 256
GC, NCH = 64, 4
RANK = 16
TAU = 16.0
NH, ND = 8, 64
NROW, GW = 4, 64
RB_R, RB_C = 15, 31
WIN = 16
MH, MD = 4, 128
DFF = 5632
FC = DFF // CH
EPS = 1e-6
MASKED = -1e30

WARM_UP = 7
RAW_SLOTS = 3
UNIT_SLOTS = 3

PQ, PK, PV, PR, NQ, NK, NV, MQ = 0, 512, 1024, 2048, 3072, 3584, 4096, 4608
PCOLS = 5120
WQ, WK, WV, WR, WG = 0, 512, 1024, 2048, 3072
WNQ, WNK, WNV, WMQ = 3104, 3616, 4128, 4640
V_ATTN, V_MEM, V_FFN, V_OUT, V_BGF, V_BGB, V_NQ, V_NK, V_MQ, V_MK, V_ROWS = 0, 16, 32, 48, 64, 68, 72, 73, 74, 75, 76

CHUNKS = [
    (False, WQ, "proj", PQ), (False, WK, "proj", PK), (False, WV, "proj", PV), (False, WV + CH, "proj", PV + CH),
    (False, WNQ, "proj", NQ), (False, WNK, "proj", NK), (True, 0, "kvm", 0), (False, WNV, "proj", NV),
    (False, WMQ, "proj", MQ), (True, CH, "kvm", CH), (False, WR, "proj", PR), (False, WR + CH, "proj", PR + CH),
]
OUT_PIECES = [(0, 8), (0, 0), (1, 8), (1, 0), (0, 4), (0, 12), (1, 4), (1, 12)] + [
    (c, k) for c in (2, 3) for k in (8, 0, 4, 12)]
U_OUT = 8 * len(CHUNKS)
U_FFN = U_OUT + 2 * len(OUT_PIECES)
U_BODY = U_FFN + 32
BODY = 24
U_TAIL = U_BODY + BODY * (FC - 2)

X_COLS = (0, 256, 512, 1024, 1536, 2048)
X_BANKS = (4, 5, 6, 7, 2, 3)
MEM_BANKS = (6, 7, 5)
DOWN_BANKS = (4, 0, 6, 4)
LAST_BANKS = (2, 0, 6, 4)

GLA_AT = [20 + 8 * h for h in range(GH)]
ATT_AT = [65 + 2 * h for h in range(NH)] + [82 + 2 * h for h in range(MH)]
NORMS = [("proj", NQ, ND, 44, 48), ("proj", NK, ND, 52, 56), ("kvm", 0, MD, 60, 65), ("proj", MQ, MD, 76, 79)]
ONORMS = [(NQ, ND, 91, 94), (MQ, MD, 100, 103)]
X1_AT = [(111, 110, 113), (115, 114, 117), (123, 122, 125), (131, 130, 133)]


def build_layer(nc, x, mem, attn_norm, w_in, wg2_f, bg_f, wg2_b, bg_b, gla_out, na_q, na_k, rpb, na_out,
                mem_norm, wkv, mem_q, mem_k, mem_out, w_out, ffn_norm, w13, w2, out):
    PADC = P
    bias_rows = nc.dram_tensor("bias_rows", [NH, RB_R, PADC], F32, kind="Internal")

    with ExitStack() as ctx:
        def sb(name, shape, dt=F32):
            return ctx.enter_context(nc.sbuf_tensor(name, shape, dt))

        def sem(name):
            return ctx.enter_context(nc.semaphore(name))

        xin = sb("xin", [P, NT, D])
        A_hi = sb("A_hi", [P, KT, T], F32R)
        A_lo = sb("A_lo", [P, KT, T], F32R)
        B_hi = sb("B_hi", [P, KT, T], F32R)
        B_lo = sb("B_lo", [P, KT, T], F32R)
        proj = sb("proj", [P, NT, PCOLS])
        kvm = sb("kvm", [P, NT, 2 * CH])
        raw = sb("raw", [P, RAW_SLOTS, 4, CH])
        w_hi = sb("w_hi", [P, UNIT_SLOTS, 2, CH], F32R)
        w_lo = sb("w_lo", [P, UNIT_SLOTS, 2, CH], F32R)
        work = sb("work", [P, 6272])
        ident = sb("ident", [P, P])
        masks = sb("masks", [P, 2, NT, P], I32)
        vrow = sb("vrow", [V_ROWS, P])
        vcol = sb("vcol", [P, V_ROWS])
        colmask = sb("colmask", [P, GW])
        resets = sb("resets", [P, 2, 2 * GC])
        small = sb("small", [P, 256])
        ps = ctx.enter_context(nc.psum_tensor("ps", [P, 8, CH], F32))

        def wk(at, n):
            return work[:, at:at + n]

        def dirs(ap):
            return ap.rearrange("p (d t) -> p d t", d=2)

        softp, la, cum, e_pos, e_neg, q_e, k_e, k_end = (dirs(wk(512 * i, 512)) for i in range(8))
        k_tok = wk(4096, 512).rearrange("p (d t k) -> p d t k", d=2, t=NT)
        states = wk(4608, 1536).rearrange("p (d n v) -> p d n v", d=2, n=3)
        scores = wk(0, 1024).rearrange("p (b t k) -> p b t k", b=2, t=NT)
        probs = wk(1024, 1024).rearrange("p (b t k) -> p b t k", b=2, t=NT)
        probsT = wk(2048, 1024).rearrange("p (b k q) -> p b k q", b=2, k=NT)
        na_qT = wk(3072, 1024).rearrange("p (j t) -> p j t", j=4)
        na_kT = wk(4608, 1024).rearrange("p (j t) -> p j t", j=4)
        osq = wk(3072, 1024).rearrange("p (t c) -> p t c", t=NT)
        h_tok = wk(0, 1024).rearrange("p (t c) -> p t c", t=NT)
        silu_g = wk(1024, 1024).rearrange("p (t c) -> p t c", t=NT)
        scoresT = sb("scoresT", [P, NT, P])
        gate_raw = proj[:, 0, PR + CH:PR + 2 * CH].rearrange("p (k c) -> p k c", c=2 * RANK)
        wg2 = proj[0:RANK, 0:2, PR:PR + CH]
        gT = proj[0:RANK, 0, MQ:MQ + CH].rearrange("p (d t) -> p d t", d=2)
        gates_raw = proj[0:4 * RANK, 1, MQ:MQ + T]
        mem_qT = proj[:, 0, 0:1024].rearrange("p (j t) -> p j t", j=4)
        mem_kT = proj[:, 1, 0:1024].rearrange("p (j t) -> p j t", j=4)
        bias = [proj[:, b, PR:PR + CH].rearrange("p (t k) -> p t k", t=NT) for b in range(2)]
        bias_rev = [proj[:, b, PR + CH:PR + 2 * CH].rearrange("p (a c) -> p a c", c=GW) for b in range(2)]
        row_scratch = kvm[:].rearrange("p t c -> p (t c)")
        psq = kvm[:, :, CH:2 * CH]
        gate_hi = B_hi[:].rearrange("p a b -> p (a b)")[:, 0:(KT + 1) * 4 * RANK]
        gate_lo = B_lo[:].rearrange("p a b -> p (a b)")[:, 0:(KT + 1) * 4 * RANK]
        pad = wk(6144, PADC)[0:NH * RB_R, :]
        rpb_sb = sb("rpb_sb", [NH * RB_R, RB_C])

        ssq_x, rstd_x = small[:, 0:2], small[:, 2:4]
        ssq_m, rstd_m = small[:, 4:6], small[:, 6:8]
        ssq_o, rstd_o = small[:, 8:16], small[:, 16:24]
        ssq_n = [small[:, 24 + 16 * i:40 + 16 * i] for i in range(6)]
        rstd_n = [small[:, 120 + 16 * i:136 + 16 * i] for i in range(6)]
        ssq_h, sum_h, rstd_h = small[:, 216:224], small[:, 224:226], small[:, 226:228]
        stat = sb("stat", [P, 128])
        negmax = stat[:, 64:68].rearrange("p (b t) -> p b t", b=2)
        psum_e = stat[:, 68:92].rearrange("p (g t) -> p g t", t=NT)
        rinv = stat[:, 92:116].rearrange("p (g t) -> p g t", t=NT)
        half = sb("half", [P, 16])

        raw_landed = [sem(f"raw_landed{i}") for i in range(RAW_SLOTS)]
        first_landed = sem("first_landed")
        hi_ready = sem("hi_ready")
        lo_ready = sem("lo_ready")
        unit_done = sem("unit_done")
        x_landed = [sem(f"x_landed{n}") for n in range(len(X_COLS) - 1)]
        mem_landed, x_again = sem("mem_landed"), sem("x_again")
        gain_landed, vec_landed = sem("gain_landed"), sem("vec_landed")
        gate_landed, wg2_landed = sem("gate_landed"), sem("wg2_landed")
        rpb_landed, rows_stored = sem("rpb_landed"), sem("rows_stored")
        rev_landed = [sem("rev_landed0"), sem("rev_landed1")]
        out_stored = sem("out_stored")
        ident_ready, pad_ready, masks_ready = sem("ident_ready"), sem("pad_ready"), sem("masks_ready")
        warm = sem("warm")
        vecT, vcol_ready = sem("vecT"), sem("vcol_ready")
        xT, xT_hi, xT_lo = sem("xT"), sem("xT_hi"), sem("xT_lo")
        mT, mT_hi, mT_lo = sem("mT"), sem("mT_hi"), sem("mT_lo")
        x_squared, m_squared = sem("x_squared"), sem("m_squared")
        rstd_x_ready, rstd_m_ready = sem("rstd_x_ready"), sem("rstd_m_ready")
        gate_hi_ready, gate_lo_ready = sem("gate_hi_ready"), sem("gate_lo_ready")
        gates_done, gates_evac, rstd_rows, gT_ready = (sem(n) for n in "gates_done gates_evac rstd_rows gT_ready".split())
        chunk_evac = sem("chunk_evac")
        g_qkT, g_z, g_abs, g_soft, g_cum, g_exp, g_gated = (sem("g_" + n) for n in
                                                            "qkT z abs soft cum exp gated".split())
        g_scores, g_kendT, g_ktok, g_masked, g_kv, g_kvx, g_state, g_o, g_oevac = (
            sem("g_" + n) for n in "scores kendT ktok masked kv kvx state o oevac".split())
        rstd_o_ready = sem("rstd_o_ready")
        n_squared, n_summed, n_rstd, n_scaled = (sem("n_" + n) for n in "squared summed rstd scaled".split())
        headT, headT_evac = sem("headT"), sem("headT_evac")
        bias_ready = sem("bias_ready")
        a_scored, a_copied, a_max, a_exp, a_pT, a_pTevac, a_pv, a_out = (
            sem("a_" + n) for n in "scored copied max exp pT pTevac pv out".split())
        y_ready, yT, yT_hi, yT_lo = sem("y_ready"), sem("yT"), sem("yT_hi"), sem("yT_lo")
        x1_squared, x1T, x1T_hi, x1T_lo = (sem("x1_" + n) for n in "squared T hi lo".split())
        sum_h_ready, rstd_h_ready = sem("sum_h_ready"), sem("rstd_h_ready")
        gate_read, h_ready, hT, hT_hi, hT_lo = (sem(n) for n in "gate_read h_ready hT hT_hi hT_lo".split())
        col_added = sem("col_added")
        act_step, dve_step, pool_step = sem("act_step"), sem("dve_step"), sem("pool_step")
        block = ctx.enter_context(nc.Block())

        def linker(eng, step):
            done = [0]

            def link(ins):
                done[0] += 1
                ins.then_inc(step, 1)
                eng.wait_ge(step, done[0])
            return link

        def acc(pair):
            return ps[:, 2 * pair:2 * pair + 2, :]

        def rows(w, r, c):
            return w[bass.ds(r, 4 * P) if not isinstance(r, int) else slice(r, r + 4 * P),
                     bass.ds(c, CH) if not isinstance(c, int) else slice(c, c + CH)].rearrange("(k p) n -> p k n", p=P)

        def gate_tiles(buf):
            v = buf.rearrange("p (k a r) -> p k a r", a=2, r=RANK)
            src = gate_raw.rearrange("p k (d r) -> p (k d) r", r=RANK).unsqueeze(2)
            return ((v[:, 0:2 * KT], src.to_broadcast([P, 2 * KT, 2, RANK])),
                    (v[:, 2 * KT:], src[:, 0:2].to_broadcast([P, 2, 2, RANK])))

        def kv_banks(h):
            pair = ((GLA_AT[h] + 8) // 8 + 1) % 2
            return 2 * pair, 2 * pair + 1

        def tok_cols(buf, col):
            return (proj if buf == "proj" else kvm)[:, :, col:col + CH]

        def groups(ap, w):
            return ap.rearrange("p t (g w) -> p t g w", w=w)

        def silu_of_gate(act):
            for t in range(NT):
                last = act.activation(silu_g[:, t, :], ps[:, t, :], ACT.Silu, scale=rstd_h[:, t:t + 1])
            last.then_inc(gate_read, 1)

        def hidden_hi(act, k0=0, bank=6):
            act.activation(B_hi[:, k0:k0 + 4, :].rearrange("p k t -> p (k t)"),
                           ps[:, bank:bank + 2, :].rearrange("p b n -> p (b n)"), ACT.Copy).then_inc(hT_hi, 1)

        def scale_groups(dve, i, ap, width):
            dve.wait_ge(n_rstd, i + 1)
            n = CH // width
            g = groups(ap, width)
            r = rstd_n[i][:, 0:NT * n].rearrange("p (t g) -> p t g", t=NT).unsqueeze(3)
            dve.tensor_tensor(g, g, r.to_broadcast([P, NT, n, width]), ALU.mult).then_inc(n_scaled, 1)

        @block.sync
        def _(sp):
            def load_x(n):
                c = slice(X_COLS[n], X_COLS[n + 1])
                sp.dma_start(xin[:, :, c], x.rearrange("(t p) n -> p t n", p=P)[:, :, c]).then_inc(x_landed[n], 16)

            for part in range(2):
                load_x(part)
                k = slice(2 * part, 2 * part + 2)
                sp.dma_start(raw[:, 0, k], rows(w_in, 0, WQ)[:, k]
                             ).then_inc((first_landed, raw_landed[0])[part], 16)
            load_x(2)

            def load(n, src, slot=None):
                s = n % RAW_SLOTS if slot is None else slot
                sp.dma_start(raw[:, s], src).then_inc(raw_landed[s], 16)

            def load_vectors():
                for row, v in ((V_MEM, mem_norm), (V_FFN, ffn_norm), (V_OUT, gla_out), (V_OUT + 8, na_out),
                               (V_OUT + 12, mem_out), (V_BGF, bg_f), (V_BGB, bg_b), (V_MQ, mem_q), (V_MK, mem_k)):
                    sp.dma_start(vrow[row:row + v.shape[1] // P, :], v.rearrange("a (k p) -> (a k) p", p=P)
                                 ).then_inc(vec_landed, 16)
                for row, v in ((V_NQ, na_q), (V_NK, na_k)):
                    for j in range(2):
                        sp.dma_start(vrow[row:row + 1, j * ND:(j + 1) * ND], v).then_inc(vec_landed, 16)

            def free(n):
                if n >= RAW_SLOTS:
                    sp.wait_ge(lo_ready, 2 * (n - RAW_SLOTS) + 2)

            n = 0
            for m, wcol, _, _ in CHUNKS:
                for k in range(4):
                    if n:
                        free(n)
                        load(n, rows(wkv if m else w_in, 4 * P * k, wcol))
                    if n == 1:
                        load_x(3)
                        load_x(4)
                    if n == 2:
                        sp.dma_start(gate_raw, w_in[:, WG:WG + 2 * RANK].rearrange("(k p) c -> p k c", p=P)
                                     ).then_inc(gate_landed, 16)
                        for d, w in enumerate((wg2_f, wg2_b)):
                            sp.dma_start(wg2[:, d, :], w).then_inc(wg2_landed, 16)
                        load_vectors()
                    n += 1
            for c, k in OUT_PIECES:
                free(n)
                load(n, rows(w_out, k * P, c * CH))
                n += 1
            for base in (0, DFF, CH, DFF + CH):
                for k in range(4):
                    free(n)
                    load(n, rows(w13, 4 * P * k, base))
                    n += 1
            with sp.Fori(1, FC - 1) as i:
                for j in range(BODY // 2):
                    sp.wait_ge(lo_ready, i * BODY + (U_BODY - BODY + 2 * (j - RAW_SLOTS) + 2))
                    if j < 4:
                        src = rows(w2, i * CH - CH, j * CH)
                    elif j < 8:
                        src = rows(w13, 4 * P * (j - 4), i * CH + CH)
                    else:
                        src = rows(w13, 4 * P * (j - 8), i * CH + (DFF + CH))
                    load(0, src, slot=(U_BODY // 2 + j) % RAW_SLOTS)
            n = U_TAIL // 2
            for chunk in (FC - 2, FC - 1):
                for c in range(4):
                    free(n)
                    load(n, rows(w2, chunk * CH, c * CH))
                    n += 1
            for c in range(4):
                for t in range(NT):
                    sp.wait_ge(col_added, 4 * FC + c + 1 + (t if c == 3 else 0))
                    sp.dma_start(out[t * P:(t + 1) * P, c * CH:(c + 1) * CH], xin[:, t, c * CH:(c + 1) * CH]
                                 ).then_inc(out_stored, 16)
            sp.wait_ge(out_stored, 16 * 4 * NT)

        @block.gpsimd
        def _(pool):
            link = linker(pool, pool_step)
            link(pool.memset(ident[:], 0.0))
            pool.affine_select(out=ident[:], in_=ident[:], compare_op=ALU.not_equal, fill=1.0, base=0,
                               pattern=[[-1, P]], channel_multiplier=1).then_inc(ident_ready, 1)
            pool.dma_start(rpb_sb[:], rpb.rearrange("h d c -> (h d) c")).then_inc(rpb_landed, 16)
            link(pool.memset(resets[:], 1.0))
            link(pool.memset(masks[:].bitcast(F32), 0.0))
            link(pool.memset(scoresT[:], 0.0))
            link(pool.memset(colmask[:], 0.0))
            link(pool.memset(pad, 0.0))
            link(pool.memset(resets[:, 0, :].rearrange("p (n c) -> p n c", c=GC)[:, :, 0:1], 0.0))
            link(pool.memset(resets[:, 1, :].rearrange("p (n c) -> p n c", c=GC)[:, :, GC - 1:GC], 0.0))
            ones = masks[:].bitcast(F32)
            for c in range(2):
                s = slice(c * GC, (c + 1) * GC)
                blk = ones[s, :, :, s]
                link(pool.memset(blk, 1.0))
                link(pool.affine_select(out=blk[:, 0], in_=blk[:, 0], compare_op=ALU.is_ge, fill=0.0, base=0,
                                        pattern=[[0, NT], [1, GC]], channel_multiplier=-1))
                link(pool.affine_select(out=blk[:, 1], in_=blk[:, 1], compare_op=ALU.is_gt, fill=0.0, base=0,
                                        pattern=[[0, NT], [-1, GC]], channel_multiplier=1))
                lowm, highm = colmask[s, 0:GW - WIN], colmask[s, WIN:GW]
                link(pool.affine_select(out=lowm, in_=lowm, compare_op=ALU.is_ge, fill=MASKED, base=WIN // 2,
                                        pattern=[[1, GW - WIN]], channel_multiplier=-1))
                link(pool.affine_select(out=highm, in_=highm, compare_op=ALU.is_ge, fill=MASKED,
                                        base=WIN // 2 - 1 - WIN, pattern=[[-1, GW - WIN]], channel_multiplier=1))
            pool.memset(half[:], -0.5).then_inc(masks_ready, 1)
            pool.wait_ge(rpb_landed, 16)
            pool.tensor_copy(pad[:, 48:48 + RB_C], rpb_sb[:, ::-1]).then_inc(pad_ready, 1)
            pool.wait_ge(pad_ready, 1)
            pool.dma_start(bias_rows[:].rearrange("h d c -> (h d) c"), pad).then_inc(rows_stored, 16)

            def inv_rms(src, dst, width, ready):
                link(pool.tensor_scalar(dst, src, 1.0 / width, EPS, ALU.mult, ALU.add))
                pool.tensor_tensor(dst, dst, half[:, 0:dst.shape[-1]], ALU.pow).then_inc(ready, 1)

            pool.wait_ge(x_squared, 2)
            inv_rms(ssq_x, rstd_x, D, rstd_x_ready)
            pool.wait_ge(m_squared, 2)
            inv_rms(ssq_m, rstd_m, D, rstd_m_ready)

            def norm(i, width):
                n = 2 * CH // width
                pool.wait_ge(n_summed, i + 1)
                inv_rms(ssq_n[i][:, 0:n], rstd_n[i][:, 0:n], width, n_rstd)

            pool.wait_ge(rows_stored, 16)

            def fetch_bias(h):
                for t in range(NT):
                    for r in range(2):
                        dr = RB_R // 2 - (2 * t + r)
                        src = bass.AP(tensor=bias_rows[:].tensor, offset=(h * RB_R + dr) * PADC,
                                      ap=[[1, GC], [PADC, NROW], [1, GW]])
                        pool.dma_start(bias_rev[h % 2][r * GC:(r + 1) * GC, t * NROW:(t + 1) * NROW, :],
                                       src).then_inc(rev_landed[h % 2], 16)

            def make_bias(h):
                pool.wait_ge(rev_landed[h % 2], 64 * (h // 2 + 1))
                if h >= 2:
                    pool.wait_ge(a_copied, h - 1)
                pool.tensor_tensor(bias[h % 2].rearrange("p t (a c) -> p (t a) c", c=GW), bias_rev[h % 2][:, :, ::-1],
                                   colmask[:].unsqueeze(1).to_broadcast([P, NT * NROW, GW]),
                                   ALU.add).then_inc(bias_ready, 1)

            norm(0, ND)
            norm(1, ND)
            pool.wait_ge(gates_done, 1)
            fetch_bias(0)
            fetch_bias(1)
            pool.wait_ge(g_z, GH)
            make_bias(0)
            make_bias(1)
            norm(2, MD)
            for h in range(2, NH):
                pool.wait_ge(bias_ready, h - 1)
                fetch_bias(h)
                make_bias(h)
                if h == 6:
                    norm(3, MD)
            pool.wait_ge(g_oevac, GH)
            inv_rms(ssq_o, rstd_o, GV, rstd_o_ready)
            norm(4, ND)
            norm(5, MD)
            pool.wait_ge(sum_h_ready, 1)
            inv_rms(sum_h, rstd_h, D, rstd_h_ready)

        @block.scalar
        def _(act):
            link = linker(act, act_step)
            act.dma_start(vrow[0:KT, :], attn_norm.rearrange("a (k p) -> (a k) p", p=P)).then_inc(gain_landed, 16)

            def split(u):
                n = u // 2
                if u == 0:
                    act.wait_ge(first_landed, 16)
                elif u % 2 == 0 or u == 1:
                    act.wait_ge(raw_landed[n % RAW_SLOTS], 16 * (n // RAW_SLOTS + 1))
                if u >= UNIT_SLOTS:
                    act.wait_ge(unit_done, u - UNIT_SLOTS + 1)
                act.activation(w_hi[:, u % UNIT_SLOTS], raw[:, u // 2 % RAW_SLOTS, 2 * (u % 2):2 * (u % 2) + 2],
                               ACT.Copy).then_inc(hi_ready, 1)

            def evac_hi(dst, bank, k0, gains, n, done):
                for k in range(n):
                    last = act.activation(dst[:, k0 + k, :], ps[:, bank + k // 2, (k % 2) * T:(k % 2 + 1) * T],
                                          ACT.Copy, scale=vcol[:, gains + k:gains + k + 1])
                last.then_inc(done, 1)

            def evac_chunk(c):
                m, _, buf, col = CHUNKS[c]
                act.wait_ge(unit_done, 8 * c + 8)
                act.wait_ge(*((rstd_m_ready, 1) if m else (rstd_x_ready, 1)))
                dst, r = tok_cols(buf, col), (rstd_m if m else rstd_x)
                if c == 9:
                    act.wait_ge(n_summed, 4)
                if c >= 10:
                    act.wait_ge(a_copied, NH)
                func = ACT.Silu if c >= 10 else ACT.Copy
                for t in range(NT):
                    last = act.activation(dst[:, t, :], acc(c % 2)[:, t, :], func, scale=r[:, t:t + 1])
                last.then_inc(chunk_evac, 1)

            act.wait_ge(ident_ready, 1)
            act.activation(stat[:, 120:121], ident[:, 0:1], ACT.Exp)
            act.wait_ge(vcol_ready, 1)
            for u in range(U_BODY):
                if u < 8:
                    act.wait_ge(xT, u + 1)
                    evac_hi(A_hi, X_BANKS[u % len(X_BANKS)], 2 * u, V_ATTN + 2 * u, 2, xT_hi)
                split(u)
                if u == 5:
                    act.wait_ge(gate_landed, 16)
                    for dst, src in gate_tiles(gate_hi):
                        last = act.activation(dst, src, ACT.Copy)
                    last.then_inc(gate_hi_ready, 1)
                if u in (8, 9):
                    t = u - 8
                    act.activation(row_scratch, xin[:, t, :], ACT.Square,
                                   accum_out=ssq_x[:, t:t + 1]).then_inc(x_squared, 1)
                    act.wait_ge(x_squared, t + 1)
                    if t == 1:
                        act.wait_ge(xT, 8)
                        act.dma_start(xin[:], mem.rearrange("(t p) n -> p t n", p=P)).then_inc(mem_landed, 16)
                if u % 8 == 3 and 11 <= u <= 99:
                    evac_chunk((u - 11) // 8)
                if u == 11:
                    act.wait_ge(gates_done, 1)
                    act.activation(gates_raw, ps[0:4 * RANK, 7, 0:T], ACT.Copy).then_inc(gates_evac, 1)
                if 17 <= u < 25:
                    b = u - 17
                    act.wait_ge(vcol_ready, 2)
                    act.wait_ge(mT, b + 1)
                    evac_hi(B_hi, MEM_BANKS[b % 3], 2 * b, V_MEM + 2 * b, 2, mT_hi)
                if u in (29, 31):
                    t = (u - 29) // 2
                    act.activation(row_scratch, xin[:, t, :], ACT.Square,
                                   accum_out=ssq_m[:, t:t + 1]).then_inc(m_squared, 1)
                    act.wait_ge(m_squared, t + 1)
                    if t == 1:
                        act.wait_ge(mT, 8)
                        act.dma_start(xin[:], x.rearrange("(t p) n -> p t n", p=P)).then_inc(x_again, 16)
                for h, at in enumerate(GLA_AT):
                    if u == at + 4:
                        act.wait_ge(g_z, h + 1)
                        if h:
                            act.wait_ge(g_cum, h)
                        for d, b in enumerate((V_BGF, V_BGB)):
                            last = act.activation(softp[:, d, :], ps[:, 5, d * T:(d + 1) * T], ACT.Abs,
                                                  bias=vcol[:, b + h:b + h + 1])
                        last.then_inc(g_abs, 1)
                        act.wait_ge(g_abs, h + 1)
                        link(act.activation(softp[:], softp[:], ACT.Exp, scale=-1.0))
                        act.activation(softp[:], softp[:], ACT.Ln, bias=1.0).then_inc(g_soft, 1)
                    if u == at + 6:
                        act.wait_ge(g_cum, h + 1)
                        if h:
                            act.wait_ge(g_state, h)
                        act.activation(e_pos[:], cum[:], ACT.Exp, scale=1.0 / TAU)
                        act.activation(e_neg[:], cum[:], ACT.Exp, scale=-1.0 / TAU).then_inc(g_exp, 1)
                    if u == at + 10:
                        act.wait_ge(g_kendT, h + 1)
                        act.activation(k_tok[:].rearrange("p d t k -> p (d t k)"), ps[:, 7, :],
                                       ACT.Copy).then_inc(g_ktok, 1)
                    if u == at + 14:
                        act.wait_ge(g_o, h + 1)
                        act.activation(proj[:, :, PV + h * GV:PV + (h + 1) * GV],
                                       ps[:, 6, :].rearrange("p (t v) -> p t v", t=NT), ACT.Copy)
                        for t in range(NT):
                            last = act.activation(k_tok[:, t].rearrange("p t k -> p (t k)"),
                                                  ps[:, 6, t * GV:(t + 1) * GV], ACT.Square,
                                                  accum_out=ssq_o[:, 2 * h + t:2 * h + t + 1])
                        last.then_inc(g_oevac, 1)
                for i, (buf, col, width, at, _) in enumerate(NORMS):
                    if u == at:
                        act.wait_ge(chunk_evac, {NQ: 5, NK: 6, 0: 7, MQ: 9}[col])
                        if i:
                            act.wait_ge(n_summed, i)
                        act.activation(psq, tok_cols(buf, col), ACT.Square).then_inc(n_squared, 1)
                for i, (col, width, at, _) in enumerate(ONORMS):
                    if u == at:
                        act.wait_ge(a_out, i + 1)
                        act.wait_ge(a_scored, NH)
                        if i:
                            act.wait_ge(n_summed, 5)
                        act.activation(osq[:], tok_cols("proj", col), ACT.Square).then_inc(n_squared, 1)
                for i, (at, dst, bank, gain) in enumerate(((61, na_qT, 4, V_NQ), (66, na_kT, 6, V_NK),
                                                           (71, mem_kT, 2, V_MK), (81, mem_qT, 0, V_MQ))):
                    if u == at:
                        act.wait_ge(headT, i + 1)
                        act.activation(dst[:, 0:2, :].rearrange("p j t -> p (j t)"), ps[:, bank, :], ACT.Copy,
                                       scale=vcol[:, gain:gain + 1]).then_inc(headT_evac, 1)
                for g, at in enumerate(ATT_AT):
                    if u == at + 4:
                        act.wait_ge(a_max, g + 1)
                        if g >= 2:
                            act.wait_ge(a_pT, g - 1)
                        for t in range(NT):
                            ins = act.activation(probs[:, g % 2, t, :], scores[:, g % 2, t, :], ACT.Exp,
                                                 bias=negmax[:, g % 2, t:t + 1], accum_out=psum_e[:, g, t:t + 1])
                            if t == 1:
                                ins.then_inc(a_exp, 1)
                    if u == at + 8:
                        act.wait_ge(a_pT, g + 1)
                        if g >= 2:
                            act.wait_ge(a_pv, g - 1)
                        act.activation(probsT[:, g % 2].rearrange("p k q -> p (k q)"), ps[:, 5, :],
                                       ACT.Copy).then_inc(a_pTevac, 1)
                for i, (at, k0, bank) in enumerate(((95, 0, 0), (97, 8, 0), (103, 4, 4), (105, 12, 6))):
                    if u == at:
                        act.wait_ge(yT, i + 1)
                        evac_hi(B_hi, bank, k0, V_OUT + k0, 4, yT_hi)
                for c, (at, _, at2) in enumerate(X1_AT):
                    if u == at + 1:
                        act.wait_ge(col_added, c + 1)
                        if c:
                            act.wait_ge(x1_squared, c)
                        for t in range(NT):
                            last = act.activation(silu_g[:, t, :], xin[:, t, c * CH:(c + 1) * CH], ACT.Square,
                                                  accum_out=ssq_h[:, 4 * t + c:4 * t + c + 1])
                        last.then_inc(x1_squared, 1)
                    if u == at2:
                        act.wait_ge(x1T, c + 1)
                        evac_hi(A_hi, 4, 4 * c, V_FFN + 4 * c, 4, x1T_hi)
                if u == U_FFN + 11:
                    act.wait_ge(unit_done, U_FFN + 8)
                    act.wait_ge(rstd_h_ready, 1)
                    silu_of_gate(act)
                if u == U_FFN + 25:
                    act.wait_ge(hT, 1)
                    hidden_hi(act)
                if u == U_FFN + 27:
                    act.wait_ge(unit_done, U_FFN + 24)
                    act.wait_ge(h_ready, 1)
                    silu_of_gate(act)

            with act.Fori(1, FC - 1) as i:
                for j in range(BODY):
                    if j % 2 == 0:
                        n = U_BODY // 2 + j // 2
                        act.wait_ge(raw_landed[n % RAW_SLOTS],
                                    i * (16 * BODY // 2 // RAW_SLOTS)
                                    + (16 * (n // RAW_SLOTS + 1) - 16 * BODY // 2 // RAW_SLOTS))
                    act.wait_ge(unit_done, i * BODY + (U_BODY - BODY + j - UNIT_SLOTS + 1))
                    act.activation(w_hi[:, (U_BODY + j) % UNIT_SLOTS],
                                   raw[:, (U_BODY + j) // 2 % RAW_SLOTS, 2 * (j % 2):2 * (j % 2) + 2],
                                   ACT.Copy).then_inc(hi_ready, 1)
                    if j == 17:
                        act.wait_ge(hT, i + 1)
                        hidden_hi(act)
                    if j == 19:
                        act.wait_ge(unit_done, i * BODY + (U_BODY - BODY + 16))
                        act.wait_ge(h_ready, i + 1)
                        silu_of_gate(act)
            for u in range(U_TAIL, U_TAIL + 16):
                split(u)
                if u == U_TAIL + 7:
                    act.wait_ge(hT, FC)
                    hidden_hi(act, k0=4, bank=2)

        @block.vector
        def _(dve):
            link = linker(dve, dve_step)

            def split(u):
                dve.wait_ge(hi_ready, u + 1)
                dve.tensor_tensor(w_lo[:, u % UNIT_SLOTS], raw[:, u // 2 % RAW_SLOTS, 2 * (u % 2):2 * (u % 2) + 2],
                                  w_hi[:, u % UNIT_SLOTS].bitcast(F32), ALU.subtract).then_inc(lo_ready, 1)

            def evac_lo(dst, high, bank, k0, gains, n, done):
                for k in range(n):
                    last = dve.scalar_tensor_tensor(dst[:, k0 + k, :], ps[:, bank + k // 2, (k % 2) * T:(k % 2 + 1) * T],
                                                    vcol[:, gains + k:gains + k + 1],
                                                    high[:, k0 + k, :].bitcast(F32), ALU.mult, ALU.subtract)
                last.then_inc(done, 1)

            dve.wait_ge(vecT, 1)
            dve.tensor_copy(vcol[:, 0:KT], ps[:, 0, 0:KT]).then_inc(vcol_ready, 1)

            def gate_times_up():
                for t in range(NT):
                    last = dve.scalar_tensor_tensor(h_tok[:, t, :], ps[:, 2 + t, :], rstd_h[:, t:t + 1],
                                                    silu_g[:, t, :], ALU.mult, ALU.mult)
                last.then_inc(h_ready, 1)

            def hidden_lo(k0=0, bank=6):
                dve.tensor_tensor(B_lo[:, k0:k0 + 4, :].rearrange("p k t -> p (k t)"),
                                  ps[:, bank:bank + 2, :].rearrange("p b n -> p (b n)"),
                                  B_hi[:, k0:k0 + 4, :].rearrange("p k t -> p (k t)").bitcast(F32),
                                  ALU.subtract).then_inc(hT_lo, 1)

            def add_down(c, bank):
                xc = xin[:, :, c * CH:(c + 1) * CH]
                dve.tensor_tensor(xc, ps[:, bank:bank + 2, :], xc, ALU.add).then_inc(col_added, 1)

            for u in range(U_BODY):
                if u < 8:
                    dve.wait_ge(xT_hi, u + 1)
                    if u == 0:
                        dve.wait_ge(vcol_ready, 1)
                    evac_lo(A_lo, A_hi, X_BANKS[u % len(X_BANKS)], 2 * u, V_ATTN + 2 * u, 2, xT_lo)
                split(u)
                if u == 6:
                    dve.wait_ge(gate_hi_ready, 1)
                    for (dst, src), (high, _) in zip(gate_tiles(gate_lo), gate_tiles(gate_hi)):
                        last = dve.tensor_tensor(dst, src, high.bitcast(F32), ALU.subtract)
                    last.then_inc(gate_lo_ready, 1)
                if u == 7:
                    dve.wait_ge(vecT, 2)
                    dve.tensor_copy(vcol[:, KT:V_ROWS], ps[:, 6, KT:V_ROWS]).then_inc(vcol_ready, 1)
                if u == 15:
                    dve.wait_ge(gates_evac, 1)
                    dve.wait_ge(rstd_rows, 1)
                    for d in range(2):
                        r = slice(2 * RANK * d, 2 * RANK * d + RANK)
                        last = dve.tensor_tensor(gT[:, d, :], gates_raw[r], ps[r, 4, 0:T], ALU.mult)
                    last.then_inc(gT_ready, 1)
                if 17 <= u < 25:
                    b = u - 17
                    dve.wait_ge(mT_hi, b + 1)
                    evac_lo(B_lo, B_hi, MEM_BANKS[b % 3], 2 * b, V_MEM + 2 * b, 2, mT_lo)
                for h, at in enumerate(GLA_AT):
                    if u == at + 4:
                        if h == 0:
                            dve.wait_ge(masks_ready, 1)
                        dve.wait_ge(g_abs, h + 1)
                        for d, b in enumerate((V_BGF, V_BGB)):
                            link(dve.tensor_scalar(la[:, d, :], ps[:, 5, d * T:(d + 1) * T],
                                                   vcol[:, b + h:b + h + 1], 0.0, ALU.add, ALU.min))
                    if u == at + 5:
                        dve.wait_ge(g_soft, h + 1)
                        link(dve.tensor_tensor(la[:], la[:], softp[:], ALU.subtract))
                        if h:
                            dve.wait_ge(g_exp, h)
                        for d, step in ((0, 1), (1, -1)):
                            for t in range(NT):
                                s = slice(t * P, (t + 1) * P)
                                last = dve.tensor_tensor_scan(cum[:, d, s][:, ::step], resets[:, d, :][:, ::step],
                                                              la[:, d, s][:, ::step], 0.0, ALU.mult, ALU.add)
                        last.then_inc(g_cum, 1)
                    if u == at + 7:
                        dve.wait_ge(g_exp, h + 1)
                        dve.wait_ge(g_qkT, h + 1)
                        if h:
                            dve.wait_ge(g_o, h)
                        for d in range(2):
                            dve.scalar_tensor_tensor(q_e[:, d, :], ps[:, 4, 0:T], GK ** -0.5, e_pos[:, d, :],
                                                     ALU.mult, ALU.mult)
                            link(dve.tensor_tensor(k_e[:, d, :], ps[:, 4, T:2 * T], e_neg[:, d, :], ALU.mult))
                        for d, edge in enumerate((GC - 1, 0)):
                            ch = lambda ap: ap.rearrange("p (n c) -> p n c", c=GC)
                            last = dve.tensor_tensor(ch(k_end[:, d, :]), ch(k_e[:, d, :]),
                                                     ch(e_pos[:, d, :])[:, :, edge:edge + 1].to_broadcast([P, NCH, GC]),
                                                     ALU.mult)
                        last.then_inc(g_gated, 1)
                    if u == at + 10:
                        dve.wait_ge(g_scores, h + 1)
                        for d in range(2):
                            ins = dve.copy_predicated(scoresT[:].rearrange("p t q -> p (t q)"),
                                                      masks[:, d].rearrange("p t q -> p (t q)"),
                                                      ps[:, 6, d * T:(d + 1) * T])
                            if d == 0:
                                link(ins)
                        ins.then_inc(g_masked, 1)
                    if u == at + 12:
                        dve.wait_ge(g_kv, h + 1)
                        f, b = kv_banks(h)
                        dve.tensor_copy(states[:, 0, 0, :], ps[:, f, 0:GV])
                        link(dve.tensor_copy(states[:, 1, 0, :], ps[:, b, GV:2 * GV]))
                        dve.scalar_tensor_tensor(states[:, 0, 1, :], states[:, 0, 0, :],
                                                 e_pos[:, 0, 2 * GC - 1:2 * GC], ps[:, b, 0:GV], ALU.mult, ALU.add)
                        link(dve.scalar_tensor_tensor(states[:, 1, 1, :], states[:, 1, 0, :],
                                                      e_pos[:, 1, 2 * GC:2 * GC + 1], ps[:, 7, 0:GV],
                                                      ALU.mult, ALU.add))
                        dve.scalar_tensor_tensor(states[:, 0, 2, :], states[:, 0, 1, :],
                                                 e_pos[:, 0, 3 * GC - 1:3 * GC], ps[:, f, GV:2 * GV], ALU.mult, ALU.add)
                        dve.wait_ge(g_kvx, h + 1)
                        dve.scalar_tensor_tensor(states[:, 1, 2, :], states[:, 1, 1, :],
                                                 e_pos[:, 1, GC:GC + 1], ps[:, 6, 0:GV],
                                                 ALU.mult, ALU.add).then_inc(g_state, 1)
                for i, (buf, col, width, at, at2) in enumerate(NORMS):
                    if u == at + 1:
                        dve.wait_ge(n_squared, i + 1)
                        dve.tensor_reduce(ssq_n[i][:, 0:2 * CH // width].rearrange("p (t g) -> p t g", t=NT),
                                          groups(psq, width), AX, ALU.add).then_inc(n_summed, 1)
                    if u == at2:
                        scale_groups(dve, i, tok_cols(buf, col), width)
                for i, (col, width, at, at2) in enumerate(ONORMS):
                    if u == at + 1:
                        dve.wait_ge(n_squared, 5 + i)
                        dve.tensor_reduce(ssq_n[4 + i][:, 0:2 * CH // width].rearrange("p (t g) -> p t g", t=NT),
                                          groups(osq[:], width), AX, ALU.add).then_inc(n_summed, 1)
                    if u == at2:
                        scale_groups(dve, 4 + i, tok_cols("proj", col), width)
                for i, (at, dst, bank, gain) in enumerate(((61, na_qT, 4, V_NQ), (66, na_kT, 6, V_NK),
                                                           (71, mem_kT, 2, V_MK), (81, mem_qT, 0, V_MQ))):
                    if u == at:
                        dve.wait_ge(headT, i + 1)
                        dve.tensor_scalar(dst[:, 2:4, :].rearrange("p j t -> p (j t)"), ps[:, bank + 1, :],
                                          vcol[:, gain:gain + 1], None, ALU.mult).then_inc(headT_evac, 1)
                for g, at in enumerate(ATT_AT):
                    if u == at + 3:
                        dve.wait_ge(a_scored, g + 1)
                        if g >= 2:
                            dve.wait_ge(a_exp, g - 1)
                        sc = ps[:, 4, :].rearrange("p (t k) -> p t k", t=NT)
                        if g < NH:
                            dve.wait_ge(bias_ready, g + 1)
                            dve.scalar_tensor_tensor(scores[:, g % 2], sc, ND ** -0.5, bias[g % 2],
                                                     ALU.mult, ALU.add).then_inc(a_copied, 1)
                        else:
                            dve.tensor_scalar(scores[:, g % 2], sc, MD ** -0.5, None, ALU.mult).then_inc(a_copied, 1)
                        dve.wait_ge(a_copied, g + 1)
                        dve.tensor_reduce(negmax[:, g % 2, :], scores[:, g % 2], AX, ALU.max,
                                          negate=True).then_inc(a_max, 1)
                for i, (at, g0, ng, w, col) in enumerate(((90, 0, NH, ND, NQ), (99, NH, MH, MD, MQ))):
                    if u == at:
                        dve.wait_ge(a_pv, g0 + ng)
                        dve.wait_ge(a_exp, g0 + ng)
                        if i == 1:
                            dve.wait_ge(headT, 4)
                        link(dve.reciprocal(rinv[:, g0:g0 + ng, :], psum_e[:, g0:g0 + ng, :]))
                        for t in range(NT):
                            last = dve.tensor_tensor(groups(tok_cols("proj", col), w)[:, t],
                                                     ps[:, 6 + t, :].rearrange("p (g w) -> p g w", w=w),
                                                     rinv[:, g0:g0 + ng, t:t + 1].to_broadcast([P, ng, w]), ALU.mult)
                        last.then_inc(a_out, 1)
                for at, c in ((92, 0), (100, 1)):
                    if u == at:
                        dve.wait_ge(chunk_evac, 11 + c)
                        dve.wait_ge(rstd_o_ready, 1)
                        for h in (2 * c, 2 * c + 1):
                            for t in range(NT):
                                o = proj[:, t, PV + h * GV:PV + (h + 1) * GV]
                                last = dve.scalar_tensor_tensor(o, o, rstd_o[:, 2 * h + t:2 * h + t + 1],
                                                                proj[:, t, PR + h * GV:PR + (h + 1) * GV],
                                                                ALU.mult, ALU.mult)
                        last.then_inc(y_ready, 1)
                for i, (at, k0, bank) in enumerate(((95, 0, 0), (97, 8, 0), (103, 4, 4), (105, 12, 6))):
                    if u == at:
                        dve.wait_ge(yT_hi, i + 1)
                        evac_lo(B_lo, B_hi, bank, k0, V_OUT + k0, 4, yT_lo)
                for c, (at, _, at2) in enumerate(X1_AT):
                    if u == at:
                        dve.wait_ge(unit_done, U_OUT + (12, 16, 24, 32)[c])
                        dve.wait_ge(x_again, 16)
                        xc = xin[:, :, c * CH:(c + 1) * CH]
                        dve.tensor_tensor(xc, acc(c % 2), xc, ALU.add).then_inc(col_added, 1)
                    if u == at2:
                        dve.wait_ge(x1T_hi, c + 1)
                        evac_lo(A_lo, A_hi, 4, 4 * c, V_FFN + 4 * c, 4, x1T_lo)
                if u == 134:
                    dve.wait_ge(x1_squared, 4)
                    dve.tensor_reduce(sum_h, ssq_h.rearrange("p (t c) -> p t c", t=NT), AX, ALU.add
                                      ).then_inc(sum_h_ready, 1)
                if u == U_FFN + 19:
                    dve.wait_ge(unit_done, U_FFN + 16)
                    dve.wait_ge(gate_read, 1)
                    gate_times_up()
                if u == U_FFN + 25:
                    dve.wait_ge(hT_hi, 1)
                    hidden_lo()

            with dve.Fori(1, FC - 1) as i:
                for j in range(BODY):
                    dve.wait_ge(hi_ready, i * BODY + (U_BODY - BODY + j + 1))
                    dve.tensor_tensor(w_lo[:, (U_BODY + j) % UNIT_SLOTS],
                                      raw[:, (U_BODY + j) // 2 % RAW_SLOTS, 2 * (j % 2):2 * (j % 2) + 2],
                                      w_hi[:, (U_BODY + j) % UNIT_SLOTS].bitcast(F32),
                                      ALU.subtract).then_inc(lo_ready, 1)
                    if j == 3:
                        dve.wait_ge(unit_done, i * BODY + (U_BODY - BODY))
                        dve.wait_ge(gate_read, i + 1)
                        gate_times_up()
                    if j in (5, 7, 9, 11):
                        c = (j - 5) // 2
                        dve.wait_ge(unit_done, i * BODY + (U_BODY - BODY + 2 + 2 * c))
                        if j == 5:
                            dve.wait_ge(x1_squared, 4)
                        dve.wait_ge(col_added, i * 4 + c)
                        add_down(c, DOWN_BANKS[c])
                    if j == 17:
                        dve.wait_ge(hT_hi, i + 1)
                        hidden_lo()
            for u in range(U_TAIL, U_TAIL + 16):
                j = u - U_TAIL
                split(u)
                if j == 3:
                    dve.wait_ge(unit_done, U_TAIL)
                    dve.wait_ge(gate_read, FC)
                    gate_times_up()
                if j == 7:
                    dve.wait_ge(hT_hi, FC)
                    hidden_lo(k0=4, bank=2)
                if j in (5, 8, 10, 12, 14):
                    c = (5, 8, 10, 12, 14).index(j)
                    dve.wait_ge(unit_done, U_TAIL + 2 + 2 * c)
                    dve.wait_ge(col_added, 4 * (FC - 1) + c)
                    add_down(c % 4, (DOWN_BANKS + LAST_BANKS)[c])
            for c in range(1, 3):
                dve.wait_ge(unit_done, U_TAIL + 10 + 2 * c)
                add_down(c, LAST_BANKS[c])
            for t in range(NT):
                dve.wait_ge(unit_done, U_TAIL + 15 + t)
                xc = xin[:, t, 3 * CH:4 * CH]
                dve.tensor_tensor(xc, ps[:, LAST_BANKS[3] + t, :], xc, ALU.add).then_inc(col_added, 1)

        @block.tensor
        def _(pe):
            def unit(hi, lo, k0, bank, s, first, last):
                for k in range(2):
                    for t in range(NT):
                        tok = slice(t * P, (t + 1) * P)
                        for n, (a, w) in enumerate(((hi, w_hi), (hi, w_lo), (lo, w_hi))):
                            mm = pe.matmul(ps[:, bank + t, :], a[:, k0 + k, tok], w[:, s, k, :],
                                           start=first and k == 0 and n == 0, stop=last and k == 1 and n == 2)
                mm.then_inc(unit_done, 1)

            def transposes(src_of, bank, n, done):
                for j in range(n):
                    for t in range(NT):
                        at = (j % 2) * T + t * P
                        last = pe.transpose(ps[:, bank + j // 2, at:at + P], src_of(j, t), ident[:])
                last.then_inc(done, 1)

            def hidden_transposes(count, bank):
                pe.wait_ge(h_ready, count)
                transposes(lambda j, t: h_tok[:, t, j * P:(j + 1) * P], bank, 4, hT)

            pe.wait_ge(ident_ready, 1)
            pe.wait_ge(gain_landed, 16)
            pe.transpose(ps[:, 0, 0:KT], vrow[0:KT, :], ident[0:KT, 0:KT]).then_inc(vecT, 1)

            def x_transposes(b):
                pe.wait_ge(x_landed[b if b < 2 else 1 + b // 2], 16)
                if b >= len(X_BANKS):
                    pe.wait_ge(xT_lo, b - len(X_BANKS) + 1)
                transposes(lambda j, t: xin[:, t, (2 * b + j) * P:(2 * b + j + 1) * P], X_BANKS[b % len(X_BANKS)], 2, xT)

            x_transposes(0)
            for n in range(WARM_UP):
                mm = pe.matmul(ps[:, 1, 0:P], ident[:], ident[:], start=n == 0, stop=n == WARM_UP - 1)
            mm.then_inc(warm, 1)
            x_transposes(1)
            pe.wait_ge(warm, 1)
            for u in range(U_BODY):
                pe.wait_ge(lo_ready, u + 1)
                if u < U_OUT:
                    c, q = u // 8, u % 8
                    if u < 8:
                        pe.wait_ge(xT_lo, u + 1)
                    if q == 0:
                        if c == 1:
                            pe.wait_ge(vcol_ready, 2)
                        if 4 <= c < 4 + GH:
                            pe.wait_ge(g_state, c - 3)
                        if c >= 2:
                            pe.wait_ge(chunk_evac, c - 1)
                        if c == 6:
                            pe.wait_ge(mT_lo, 8)
                        if c == 9:
                            pe.wait_ge(headT_evac, 6)
                        if c == 10:
                            pe.wait_ge(headT_evac, 8)
                    m = CHUNKS[c][0]
                    unit(B_hi if m else A_hi, B_lo if m else A_lo, 2 * q, 2 * (c % 2), u % UNIT_SLOTS, q == 0, q == 7)
                elif u < U_FFN:
                    c, k0 = OUT_PIECES[(u - U_OUT) // 2]
                    k = k0 + 2 * (u % 2)
                    if u == U_OUT:
                        pe.wait_ge(yT_lo, 2)
                    if u == U_OUT + 4:
                        pe.wait_ge(chunk_evac, 12)
                    if u == U_OUT + 8:
                        pe.wait_ge(yT_lo, 3)
                    if u == U_OUT + 10:
                        pe.wait_ge(yT_lo, 4)
                    if u == U_OUT + 16:
                        pe.wait_ge(col_added, 1)
                    if u == U_OUT + 24:
                        pe.wait_ge(col_added, 2)
                    unit(B_hi, B_lo, k, 2 * (c % 2), u % UNIT_SLOTS, k == 8, k == 14)
                else:
                    q = (u - U_FFN) % 8
                    if u == U_FFN:
                        pe.wait_ge(col_added, 3)
                        pe.wait_ge(x1T_lo, 3)
                    if u == U_FFN + 6:
                        pe.wait_ge(x1T_lo, 4)
                    if u == U_FFN + 8:
                        pe.wait_ge(col_added, 4)
                    if u == U_FFN + 16:
                        pe.wait_ge(gate_read, 1)
                    if u == U_FFN + 24:
                        pe.wait_ge(h_ready, 1)
                    unit(A_hi, A_lo, 2 * q, 2 * ((u - U_FFN) // 8 % 2), u % UNIT_SLOTS, q == 0, q == 7)

                if u < 5:
                    for b in ((2, 3), (4,), (5,), (6,), (7,))[u]:
                        x_transposes(b)
                if u == 4:
                    pe.wait_ge(vec_landed, 16 * 13)
                    pe.wait_ge(xT_lo, 3)
                    pe.transpose(ps[:, 6, 0:V_ROWS], vrow[:], ident[0:V_ROWS, 0:V_ROWS]).then_inc(vecT, 1)
                if u == 7:
                    pe.wait_ge(gate_lo_ready, 1)
                    pe.wait_ge(xT_lo, 8)
                    for k in range(KT):
                        for n, (w, a) in enumerate(((gate_hi, A_hi), (gate_lo, A_hi), (gate_hi, A_lo))):
                            mm = pe.matmul(ps[:, 7, 0:T], w[:, 4 * RANK * k:4 * RANK * k + P], a[:, k, :],
                                           start=k == 0 and n == 0, stop=k == KT - 1 and n == 2)
                    mm.then_inc(gates_done, 1)
                if u == 11:
                    pe.wait_ge(rstd_x_ready, 1)
                    for t in range(NT):
                        last = pe.matmul(ps[:, 4, t * P:(t + 1) * P], rstd_x[:, t:t + 1].to_broadcast([P, P]), ident[:],
                                         start=True, stop=True)
                    last.then_inc(rstd_rows, 1)
                if 13 <= u < 21:
                    b = u - 13
                    if b == 0:
                        pe.wait_ge(mem_landed, 16)
                    if b >= 3:
                        pe.wait_ge(mT_lo, b - 2)
                    transposes(lambda j, t: xin[:, t, (2 * b + j) * P:(2 * b + j + 1) * P], MEM_BANKS[b % 3], 2, mT)
                for h, at in enumerate(GLA_AT):
                    if u == at:
                        pe.wait_ge(chunk_evac, 2)
                        pe.wait_ge(gT_ready, 1)
                        pe.wait_ge(mT_lo, 6)
                        if h:
                            pe.wait_ge(g_gated, h)
                        for j, col in enumerate((PQ, PK)):
                            for t in range(NT):
                                last = pe.transpose(ps[:, 4, j * T + t * P:j * T + (t + 1) * P],
                                                    proj[:, t, col + h * GK:col + (h + 1) * GK], ident[:])
                        last.then_inc(g_qkT, 1)
                        pe.wait_ge(wg2_landed, 32)
                        for d in range(2):
                            last = pe.matmul(ps[:, 5, d * T:(d + 1) * T], wg2[:, d, h * GK:(h + 1) * GK], gT[:, d, :],
                                             start=True, stop=True)
                        last.then_inc(g_z, 1)
                    if u == at + 7:
                        pe.wait_ge(g_gated, h + 1)
                        pe.wait_ge(mT_lo, 8)
                        if h:
                            pe.wait_ge(g_oevac, h)
                        for d in range(2):
                            for t in range(NT):
                                s = slice(t * P, (t + 1) * P)
                                last = pe.matmul(ps[:, 6, d * T + t * P:d * T + (t + 1) * P], k_e[:, d, s],
                                                 q_e[:, d, s], start=True, stop=True)
                        last.then_inc(g_scores, 1)
                        for d in range(2):
                            for t in range(NT):
                                at2 = (2 * d + t) * P
                                last = pe.transpose(ps[:, 7, at2:at2 + P], k_end[:, d, t * P:(t + 1) * P], ident[:])
                        last.then_inc(g_kendT, 1)
                    if u == at + 8:
                        pe.wait_ge(g_ktok, h + 1)
                        pe.wait_ge(chunk_evac, 3 + h)
                        f, b = kv_banks(h)
                        for d, n, bank, half_ in ((0, 0, f, 0), (0, 1, b, 0), (0, 2, f, 1), (1, 3, b, 1), (1, 2, 7, 0)):
                            r = slice((n % 2) * GC, (n % 2 + 1) * GC)
                            last = pe.matmul(ps[:, bank, half_ * GV:(half_ + 1) * GV], k_tok[r, d, n // 2, :],
                                             proj[r, n // 2, PV + h * GV:PV + (h + 1) * GV], start=True, stop=True)
                        last.then_inc(g_kv, 1)
                        pe.wait_ge(g_masked, h + 1)
                        pe.matmul(ps[:, 6, 0:GV], k_tok[GC:P, 1, 0, :], proj[GC:P, 0, PV + h * GV:PV + (h + 1) * GV],
                                  start=True, stop=True).then_inc(g_kvx, 1)
                    if u == at + 11:
                        pe.wait_ge(g_state, h + 1)
                        for t in range(NT):
                            o = ps[:, 6, t * GV:(t + 1) * GV]
                            terms = [(1, 0, 2), (0, 1, 0), (1, 1, 1)] if t == 0 else [(0, 2, 1), (0, 3, 2), (1, 2, 0)]
                            for k, (d, n, s) in enumerate(terms):
                                r = slice((n % 2) * GC, (n % 2 + 1) * GC)
                                pe.matmul(o[r, :], q_e[:, d, n * GC:(n + 1) * GC], states[:, d, s, :],
                                          start=k < 2, stop=False, skip_group_check=True)
                            last = pe.matmul(o, scoresT[:, t, :], proj[:, t, PV + h * GV:PV + (h + 1) * GV],
                                             start=False, stop=True, skip_group_check=True)
                        last.then_inc(g_o, 1)
                for i, (at, buf, col, bank, scaled) in enumerate(((57, "proj", NQ, 4, 1), (62, "proj", NK, 6, 2),
                                                                  (68, "kvm", 0, 2, 3), (78, "proj", MQ, 0, 4))):
                    if u == at:
                        pe.wait_ge(n_scaled, scaled)
                        if i == 0:
                            pe.wait_ge(g_state, GH)
                        if i == 1:
                            pe.wait_ge(g_oevac, GH)
                        if i == 2:
                            pe.wait_ge(chunk_evac, 8)
                        if i == 3:
                            pe.wait_ge(chunk_evac, 9)
                        transposes(lambda j, t: tok_cols(buf, col)[:, t, j * P:(j + 1) * P], bank, 4, headT)
                for g, at in enumerate(ATT_AT):
                    if u == at:
                        if g == 0:
                            pe.wait_ge(headT_evac, 4)
                        else:
                            pe.wait_ge(a_copied, g)
                        if g == NH:
                            pe.wait_ge(headT_evac, 8)
                        for t in range(NT):
                            q = slice(t * P, (t + 1) * P)
                            if g < NH:
                                r = slice((g % 2) * ND, (g % 2 + 1) * ND)
                                lhs, rhs = na_qT[r, g // 2, q], na_kT[r, g // 2, :]
                            else:
                                lhs, rhs = mem_qT[:, g - NH, q], mem_kT[:, g - NH, :]
                            last = pe.matmul(ps[:, 4, t * T:(t + 1) * T], lhs, rhs, start=True, stop=True)
                        last.then_inc(a_scored, 1)
                    if u == at + 4:
                        pe.wait_ge(a_exp, g + 1)
                        if g:
                            pe.wait_ge(a_pTevac, g)
                        for k in range(NT):
                            for t in range(NT):
                                last = pe.transpose(ps[:, 5, k * T + t * P:k * T + (t + 1) * P],
                                                    probs[:, g % 2, t, k * P:(k + 1) * P], ident[:])
                        last.then_inc(a_pT, 1)
                    if u == at + 7:
                        pe.wait_ge(a_pTevac, g + 1)
                        if g == 0:
                            pe.wait_ge(chunk_evac, 8)
                        if g == NH:
                            pe.wait_ge(chunk_evac, 10)
                            pe.wait_ge(a_out, 1)
                        w = ND if g < NH else MD
                        h = g if g < NH else g - NH
                        v = proj[:, :, NV:NV + CH] if g < NH else kvm[:, :, CH:2 * CH]
                        for t in range(NT):
                            for k in range(NT):
                                last = pe.matmul(ps[:, 6 + t, h * w:(h + 1) * w], probsT[:, g % 2, k, t * P:(t + 1) * P],
                                                 v[:, k, h * w:(h + 1) * w], start=k == 0, stop=k == NT - 1)
                        last.then_inc(a_pv, 1)
                for i, (at, col, bank) in enumerate(((92, PV, 0), (94, NQ, 0), (100, PV + CH, 4), (102, MQ, 6))):
                    if u == at:
                        if i == 0:
                            pe.wait_ge(y_ready, 1)
                            pe.wait_ge(chunk_evac, 11)
                        if i == 1:
                            pe.wait_ge(n_scaled, 5)
                            pe.wait_ge(yT_lo, 1)
                        if i == 2:
                            pe.wait_ge(y_ready, 2)
                        if i == 3:
                            pe.wait_ge(n_scaled, 6)
                        transposes(lambda j, t: proj[:, t, col + j * P:col + (j + 1) * P], bank, 4, yT)
                for c, (_, at, _) in enumerate(X1_AT):
                    if u == at:
                        pe.wait_ge(col_added, c + 1)
                        pe.wait_ge(x1T_lo, c) if c else pe.wait_ge(yT_lo, 3)
                        transposes(lambda j, t: xin[:, t, c * CH + j * P:c * CH + (j + 1) * P], 4, 4, x1T)

                if u == U_FFN + 21:
                    hidden_transposes(1, 6)

            with pe.Fori(1, FC - 1) as i:
                for j in range(BODY):
                    pe.wait_ge(lo_ready, i * BODY + (U_BODY - BODY + j + 1))
                    s = (U_BODY + j) % UNIT_SLOTS
                    if j < 8:
                        c, k = j // 2, 2 * (j % 2)
                        if j == 0:
                            pe.wait_ge(hT_lo, i)
                            pe.wait_ge(col_added, i * 4)
                        if j == 2:
                            pe.wait_ge(gate_read, i + 1)
                        if j == 6:
                            pe.wait_ge(col_added, i * 4 + 1)
                        unit(B_hi, B_lo, k, DOWN_BANKS[c], s, k == 0, k == 2)
                    elif j < 16:
                        if j == 8:
                            pe.wait_ge(col_added, i * 4 + 2)
                        unit(A_hi, A_lo, 2 * (j - 8), 0, s, j == 8, j == 15)
                    else:
                        if j == 16:
                            pe.wait_ge(h_ready, i + 1)
                        unit(A_hi, A_lo, 2 * (j - 16), 2, s, j == 16, j == 23)
                    if j == 13:
                        pe.wait_ge(col_added, i * 4 + 3)
                        hidden_transposes(i + 1, 6)
            for j in range(14):
                c, k = j // 2 % 4, 2 * (j % 2)
                last_chunk = j >= 8
                pe.wait_ge(lo_ready, U_TAIL + j + 1)
                if j == 0:
                    pe.wait_ge(hT_lo, FC - 1)
                    pe.wait_ge(col_added, 4 * (FC - 1))
                if j == 2:
                    pe.wait_ge(gate_read, FC)
                if j == 6:
                    pe.wait_ge(col_added, 4 * (FC - 1) + 1)
                if j == 8:
                    pe.wait_ge(hT_lo, FC)
                if j > 8 and k == 0:
                    pe.wait_ge(col_added, 4 * (FC - 1) + c + 1)
                unit(B_hi, B_lo, k + 4 * last_chunk, (LAST_BANKS if last_chunk else DOWN_BANKS)[c],
                     (U_TAIL + j) % UNIT_SLOTS, k == 0, k == 2)
                if j == 4:
                    hidden_transposes(FC, 2)
            pe.wait_ge(lo_ready, U_TAIL + 16)
            pe.wait_ge(col_added, 4 * FC)
            for t in range(NT):
                tok = slice(t * P, (t + 1) * P)
                for k in range(4):
                    s = (U_TAIL + 14 + k // 2) % UNIT_SLOTS
                    for n, (a, w) in enumerate(((B_hi, w_hi), (B_hi, w_lo), (B_lo, w_hi))):
                        mm = pe.matmul(ps[:, LAST_BANKS[3] + t, :], a[:, 4 + k, tok], w[:, s, k % 2, :],
                                       start=k == 0 and n == 0, stop=k == 3 and n == 2)
                mm.then_inc(unit_done, 1)


_INS = ["x", "mem", "attn_norm", "w_in", "gla_wg2_f", "gla_bg_f", "gla_wg2_b", "gla_bg_b", "gla_out_norm",
        "na_q_norm", "na_k_norm", "na_rpb", "na_out_norm", "mem_norm", "mem_wkv", "mem_q_norm", "mem_k_norm",
        "mem_out_norm", "w_out", "ffn_norm", "ffn_w13", "ffn_w2"]
_SQUEEZE = {"x", "mem", "w_in", "gla_wg2_f", "gla_wg2_b", "na_rpb", "mem_wkv", "w_out", "ffn_w13", "ffn_w2"}


def kernel(**inputs):
    import numpy as _np
    import concourse.bacc as _bacc
    from concourse import mybir as _mybir
    from concourse.bass_utils import run_bass_kernel_spmd as _run

    nc = _bacc.Bacc("TRN2", target_bir_lowering=False, num_devices=1)
    arrays, args = {}, []
    for name in _INS:
        a = _np.ascontiguousarray(inputs[name])
        if name in _SQUEEZE:
            a = a.reshape(a.shape[1:])
        arrays[f"in_{name}_dram"] = a
        args.append(nc.dram_tensor(f"in_{name}_dram", a.shape, _mybir.dt.from_np(a.dtype), kind="ExternalInput").ap())
    out = nc.dram_tensor("out_0_dram", (T, D), F32, kind="ExternalOutput").ap()
    build_layer(nc, *args, out)
    r = _run(nc, [arrays], core_ids=[0])
    return r.results[0]["out_0_dram"].reshape(1, T, D)
```
